# Optimizing a Trainium2 kernel written in Bass

```python
import math
import jax
import jax.numpy as jnp
from jax import lax
import numpy as np

D_MODEL = 1024
BATCH = 1
SEQ = 512
DEPTH = 1
DEC_BATCH = 8
DEC_SEQ = 1
PAST_LEN = 4096
PAGE_SIZE = 128

MIX_WIDTH = D_MODEL
ATTN_WIDTH = MIX_WIDTH // 2
CONV_CH = MIX_WIDTH - ATTN_WIDTH
DIFF_HEADS = 4
V_DIM = ATTN_WIDTH // DIFF_HEADS
QK_DIM = V_DIM // 2
QK_COLS = DIFF_HEADS * 2 * QK_DIM
IN_COLS = 2 * QK_COLS + ATTN_WIDTH + 2 * CONV_CH
CONV_K = 31
ROPE_THETA = 10000.0
Q_BLOCK = 128
N_EXPERTS = 32
TOP_K = 4
D_FF = D_MODEL
SWIGLU_LIMIT = 7.0
SWIGLU_ALPHA = 1.702
EPS = 1e-6
NEG = -1e30

kernel_name = "hymba_conformer_diffattn_moe_step"

def _rmsnorm(x, w):
    xf = x.astype(jnp.float32)
    y = xf * lax.rsqrt(jnp.mean(xf * xf, axis=-1, keepdims=True) + EPS)
    return (y * w.astype(jnp.float32)).astype(x.dtype)

def _layernorm(x, g, b):
    xf = x.astype(jnp.float32)
    mu = jnp.mean(xf, axis=-1, keepdims=True)
    xc = xf - mu
    y = xc * lax.rsqrt(jnp.mean(xc * xc, axis=-1, keepdims=True) + EPS)
    return (y * g.astype(jnp.float32) + b.astype(jnp.float32)).astype(x.dtype)

def _rope(x, pos):
    half = QK_DIM // 2
    inv = jnp.power(ROPE_THETA, -jnp.arange(half, dtype=jnp.float32) / half)
    ang = pos[:, None] * inv[None, :]
    cos = jnp.cos(ang)[None, :, None, None, :]
    sin = jnp.sin(ang)[None, :, None, None, :]
    xf = x.astype(jnp.float32)
    x1, x2 = xf[..., :half], xf[..., half:]
    return jnp.concatenate([x1 * cos - x2 * sin, x2 * cos + x1 * sin], axis=-1).astype(x.dtype)

def _project(x, pos, norm1_w, w_in, q_norm_w, k_norm_w):
    B, S, _ = x.shape
    h = _rmsnorm(x, norm1_w)
    p = h @ w_in
    q = p[..., :QK_COLS].reshape(B, S, DIFF_HEADS, 2, QK_DIM)
    k = p[..., QK_COLS:2 * QK_COLS].reshape(B, S, DIFF_HEADS, 2, QK_DIM)
    v = p[..., 2 * QK_COLS:2 * QK_COLS + ATTN_WIDTH].reshape(B, S, DIFF_HEADS, V_DIM)
    ua = p[..., IN_COLS - 2 * CONV_CH:IN_COLS - CONV_CH]
    ub = p[..., IN_COLS - CONV_CH:]
    u = ua * jax.nn.sigmoid(ub)
    q = _rope(_rmsnorm(q, q_norm_w), pos)
    k = _rope(_rmsnorm(k, k_norm_w), pos)
    return q, k, v, u

def _lambda(lq1, lk1, lq2, lk2, lam_init):
    f = jnp.float32
    return (jnp.exp(jnp.sum(lq1.astype(f) * lk1.astype(f)))
            - jnp.exp(jnp.sum(lq2.astype(f) * lk2.astype(f))) + lam_init)

def _scores(q, k):
    s = jnp.einsum('bqhcd,bkhcd->bhcqk', q, k, preferred_element_type=jnp.float32)
    return s * (QK_DIM ** -0.5)

def _diff_weights(s, lam):
    p = jax.nn.softmax(s, axis=-1)
    return p[:, :, 0] - lam * p[:, :, 1]

def _diff_attn_prompt(q, k, v, lam):
    B, S = q.shape[0], q.shape[1]
    nb = S // Q_BLOCK
    qb = jnp.moveaxis(q.reshape(B, nb, Q_BLOCK, DIFF_HEADS, 2, QK_DIM), 1, 0)
    vf = v.astype(jnp.float32)
    kpos = jnp.arange(S)

    def block(args):
        qblk, i = args
        qpos = i * Q_BLOCK + jnp.arange(Q_BLOCK)
        s = jnp.where(kpos[None, :] <= qpos[:, None], _scores(qblk, k), NEG)
        a = _diff_weights(s, lam)
        return jnp.einsum('bhqk,bkhd->bqhd', a, vf)

    o = lax.map(block, (qb, jnp.arange(nb)))
    return jnp.moveaxis(o, 0, 1).reshape(B, S, DIFF_HEADS, V_DIM)

def _diff_attn_sample(q, k_new, v_new, k_past, v_past, lam):
    sq = q.shape[1]
    n_past = k_past.shape[1]
    causal = jnp.arange(sq)[None, :] <= jnp.arange(sq)[:, None]
    s = jnp.concatenate([_scores(q, k_past), jnp.where(causal, _scores(q, k_new), NEG)], axis=-1)
    a = _diff_weights(s, lam)
    o_past = jnp.einsum('bhqk,bkhd->bqhd', a[..., :n_past], v_past.astype(jnp.float32))
    o_new = jnp.einsum('bhqk,bkhd->bqhd', a[..., n_past:], v_new.astype(jnp.float32))
    return o_past + o_new

def _diff_head_out(o, subln_w, lam_init, dtype):
    B, S = o.shape[0], o.shape[1]
    o = _rmsnorm(o, subln_w) * (1.0 - lam_init)
    return o.reshape(B, S, ATTN_WIDTH).astype(dtype)

def _conv_mixer(u_ext, conv_w, conv_b, ln_g, ln_b):
    y = lax.conv_general_dilated(u_ext, conv_w[:, None, :].astype(u_ext.dtype),
                                 window_strides=(1,), padding='VALID',
                                 dimension_numbers=('NWC', 'WIO', 'NWC'),
                                 feature_group_count=CONV_CH)
    y = y + conv_b.astype(y.dtype)
    return jax.nn.silu(_layernorm(y, ln_g, ln_b))

def _moe(h, router_w, router_b, w_gate_up, b_gate_up, w_down, b_down):
    T, D = h.shape
    logits = (h @ router_w).astype(jnp.float32) + router_b.astype(jnp.float32)
    top_vals, top_idx = lax.top_k(logits, TOP_K)
    gates = jax.nn.softmax(top_vals, axis=-1)
    n_assign = T * TOP_K
    blk = max(8, min(256, n_assign // N_EXPERTS))
    n_blocks = -(-n_assign // blk) + N_EXPERTS
    flat_e = top_idx.reshape(-1).astype(jnp.int32)
    order = jnp.argsort(flat_e)
    sorted_e = flat_e[order]
    tok = (order // TOP_K).astype(jnp.int32)
    counts = jnp.bincount(flat_e, length=N_EXPERTS).astype(jnp.int32)
    padded = (counts + blk - 1) // blk * blk
    pad_end = jnp.cumsum(padded)
    pad_start = pad_end - padded
    start = jnp.cumsum(counts) - counts
    dest = pad_start[sorted_e] + jnp.arange(n_assign, dtype=jnp.int32) - start[sorted_e]
    row_tok = jnp.zeros((n_blocks * blk,), jnp.int32).at[dest].set(tok)
    xs = h[row_tok].reshape(n_blocks, blk, D)
    blk_e = jnp.minimum(jnp.searchsorted(pad_end, jnp.arange(n_blocks, dtype=jnp.int32) * blk,
                                         side='right'), N_EXPERTS - 1)

    def expert_block(args):
        xb, e = args
        gu = xb @ w_gate_up[e] + b_gate_up[e]
        g = jnp.minimum(gu[:, :D_FF], SWIGLU_LIMIT)
        u = jnp.clip(gu[:, D_FF:], -SWIGLU_LIMIT, SWIGLU_LIMIT)
        act = (u + 1) * g * jax.nn.sigmoid(SWIGLU_ALPHA * g)
        return act @ w_down[e] + b_down[e]

    ys = lax.map(expert_block, (xs, blk_e)).reshape(n_blocks * blk, D)
    contrib = ys[dest].astype(jnp.float32) * gates.reshape(-1)[order][:, None]
    return jax.ops.segment_sum(contrib, tok, num_segments=T).astype(h.dtype)

def _layer_tail(x, attn, conv, w_out, norm2_w, router_w, router_b, w_gate_up, b_gate_up, w_down, b_down):
    B, S, D = x.shape
    x = x + jnp.concatenate([attn, conv], axis=-1) @ w_out
    h = _rmsnorm(x, norm2_w).reshape(B * S, D)
    return x + _moe(h, router_w, router_b, w_gate_up, b_gate_up, w_down, b_down).reshape(B, S, D)

def setup_inputs(seed: int = 0) -> dict:
    key = jax.random.key(seed)
    it = iter(list(jax.random.split(key, 32)))
    f32 = jnp.float32

    def nrm(shape, scale):
        return scale * jax.random.normal(next(it), shape, f32)

    n_pages = PAST_LEN // PAGE_SIZE
    n_used = DEC_BATCH * n_pages
    n_phys = n_used + max(1, n_used // 4)
    x_prompt = nrm((BATCH, SEQ, D_MODEL), 1.0)
    x_sample = nrm((DEC_BATCH, DEC_SEQ, D_MODEL), 1.0)
    cache_k = nrm((DEPTH, n_phys, PAGE_SIZE, DIFF_HEADS, 2, QK_DIM), 1.0)
    cache_v = nrm((DEPTH, n_phys, PAGE_SIZE, DIFF_HEADS, V_DIM), 1.0)
    state_conv = nrm((DEPTH, DEC_BATCH, CONV_K - 1, CONV_CH), 0.5)
    page_table = jax.random.permutation(next(it), n_phys)[:n_used].reshape(DEC_BATCH, n_pages).astype(jnp.int32)
    return {
        "x_prompt": x_prompt,
        "x_sample": x_sample,
        "cache_k": cache_k,
        "cache_v": cache_v,
        "state_conv": state_conv,
        "page_table": page_table,
        "norm1_w": 1.0 + nrm((DEPTH, D_MODEL), 0.02),
        "w_in": nrm((DEPTH, D_MODEL, IN_COLS), D_MODEL ** -0.5),
        "q_norm_w": 1.0 + nrm((DEPTH, QK_DIM), 0.02),
        "k_norm_w": 1.0 + nrm((DEPTH, QK_DIM), 0.02),
        "lambda_q1": nrm((DEPTH, QK_DIM), 0.1),
        "lambda_k1": nrm((DEPTH, QK_DIM), 0.1),
        "lambda_q2": nrm((DEPTH, QK_DIM), 0.1),
        "lambda_k2": nrm((DEPTH, QK_DIM), 0.1),
        "subln_w": 1.0 + nrm((DEPTH, V_DIM), 0.02),
        "conv_w": nrm((DEPTH, CONV_K, CONV_CH), CONV_K ** -0.5),
        "conv_b": nrm((DEPTH, CONV_CH), 0.01),
        "conv_ln_g": 1.0 + nrm((DEPTH, CONV_CH), 0.02),
        "conv_ln_b": nrm((DEPTH, CONV_CH), 0.01),
        "w_out": nrm((DEPTH, MIX_WIDTH, D_MODEL), MIX_WIDTH ** -0.5),
        "norm2_w": 1.0 + nrm((DEPTH, D_MODEL), 0.02),
        "router_w": nrm((DEPTH, D_MODEL, N_EXPERTS), D_MODEL ** -0.5),
        "router_b": nrm((DEPTH, N_EXPERTS), 0.01),
        "w_gate_up": nrm((DEPTH, N_EXPERTS, D_MODEL, 2 * D_FF), D_MODEL ** -0.5),
        "b_gate_up": nrm((DEPTH, N_EXPERTS, 2 * D_FF), 0.01),
        "w_down": nrm((DEPTH, N_EXPERTS, D_FF, D_MODEL), D_FF ** -0.5),
        "b_down": nrm((DEPTH, N_EXPERTS, D_MODEL), 0.01),
    }

def reference(x_prompt, x_sample, cache_k, cache_v, state_conv, page_table, norm1_w, w_in,
              q_norm_w, k_norm_w, lambda_q1, lambda_k1, lambda_q2, lambda_k2, subln_w,
              conv_w, conv_b, conv_ln_g, conv_ln_b, w_out, norm2_w, router_w, router_b,
              w_gate_up, b_gate_up, w_down, b_down):
    bs, ss = x_sample.shape[0], x_sample.shape[1]
    n_past = page_table.shape[1] * cache_k.shape[2]
    pos_p = jnp.arange(x_prompt.shape[1], dtype=jnp.float32)
    pos_s = n_past + jnp.arange(ss, dtype=jnp.float32)
    xp, xs = x_prompt, x_sample
    kp_l, vp_l, cp_l, ks_l, vs_l, cs_l = [], [], [], [], [], []
    for l in range(DEPTH):
        lam_init = 0.8 - 0.6 * math.exp(-0.3 * l)
        lam = _lambda(lambda_q1[l], lambda_k1[l], lambda_q2[l], lambda_k2[l], lam_init)
        tail = (w_out[l], norm2_w[l], router_w[l], router_b[l], w_gate_up[l], b_gate_up[l], w_down[l], b_down[l])
        conv_p = (conv_w[l], conv_b[l], conv_ln_g[l], conv_ln_b[l])

        q, k, v, u = _project(xp, pos_p, norm1_w[l], w_in[l], q_norm_w[l], k_norm_w[l])
        attn = _diff_head_out(_diff_attn_prompt(q, k, v, lam), subln_w[l], lam_init, xp.dtype)
        u_ext = jnp.pad(u, ((0, 0), (CONV_K - 1, 0), (0, 0)))
        conv = _conv_mixer(u_ext, *conv_p)
        xp = _layer_tail(xp, attn, conv, *tail)
        kp_l.append(k)
        vp_l.append(v)
        cp_l.append(u_ext[:, -(CONV_K - 1):])

        q, k, v, u = _project(xs, pos_s, norm1_w[l], w_in[l], q_norm_w[l], k_norm_w[l])
        k_past = cache_k[l][page_table].reshape(bs, n_past, DIFF_HEADS, 2, QK_DIM)
        v_past = cache_v[l][page_table].reshape(bs, n_past, DIFF_HEADS, V_DIM)
        attn = _diff_head_out(_diff_attn_sample(q, k, v, k_past, v_past, lam), subln_w[l], lam_init, xs.dtype)
        u_ext = jnp.concatenate([state_conv[l].astype(u.dtype), u], axis=1)
        conv = _conv_mixer(u_ext, *conv_p)
        xs = _layer_tail(xs, attn, conv, *tail)
        ks_l.append(k)
        vs_l.append(v)
        cs_l.append(u_ext[:, -(CONV_K - 1):])

    new_k_prompt = jnp.stack(kp_l)
    new_v_prompt = jnp.stack(vp_l)
    new_conv_prompt = jnp.stack(cp_l)
    new_k_sample = jnp.stack(ks_l)
    new_v_sample = jnp.stack(vs_l)
    new_conv_sample = jnp.stack(cs_l)
    return (xp, xs, new_k_prompt, new_v_prompt, new_conv_prompt, new_k_sample, new_v_sample, new_conv_sample)


_drawn_inputs = setup_inputs


def setup_inputs(seed=0):
    import zlib

    import numpy as np

    out = dict(_drawn_inputs(seed))
    spreads = {}
    factors = {'b_gate_up': 8.0, 'b_down': 8.0}
    for name, (base, spread) in spreads.items():
        noise = np.random.default_rng([zlib.crc32(name.encode()), seed]).standard_normal(out[name].shape)
        drawn = base * np.exp(spread * noise) if base else spread * noise
        out[name] = jnp.asarray(drawn.astype(out[name].dtype))
    for name, factor in factors.items():
        out[name] = (out[name] * factor).astype(out[name].dtype)
    return out
```

```python
import math
import numpy as np
import concourse.bass as bass
from concourse import mybir
from contextlib import ExitStack

P = 128
D = 1024
KT = D // P
SEQ, NB = 512, 8
TOK = SEQ + NB
TILES = SEQ // P
H, C, QD, VD = 4, 2, 64, 128
HC = H * C
AW = H * VD
CH = 512
CT = CH // P
TAPS = 31
PAGES, PAGE = 32, 128
GP = 2
NG = PAGES // GP
RING = 4
IN_COLS = 2560
E, TOPK, F = 32, 4, 1024
PAIRS = TOK * TOPK
CAP = P
OVF = PAIRS // CAP
BLOCKS = E + OVF
TCOLS = BLOCKS + 1
UNUSED = 1 << 20
LIMIT, ALPHA = 7.0, 1.702
EPS = 1e-6
NEG = -1e30
SM_SCALE = QD ** -0.5
LAM_INIT = 0.8 - 0.6 * math.exp(0.0)


class Chain:

    def __init__(self, eng, sem, base=0):
        self.eng, self.sem, self.base, self.n = eng, sem, base, 0

    def link(self, ins):
        self.n += 1
        ins.then_inc(self.sem, 1)
        self.eng.wait_ge(self.sem, self.base + self.n)


def hybrid_step(nc, x_prompt, x_sample, cache_k, cache_v, state_conv, page_table, norm1_w, w_in,
                q_norm_w, k_norm_w, lambda_q1, lambda_k1, lambda_q2, lambda_k2, subln_w, conv_w,
                conv_b, conv_ln_g, conv_ln_b, w_out, norm2_w, router_w, router_b, w_gate_up,
                b_gate_up, w_down, b_down, rope_table,
                y_prompt, y_sample, new_k_p, new_v_p, new_conv_p, new_k_s, new_v_s, new_conv_s,
                h2_rows, x2_rows, y_rows, q_rows, s_new_rows, slot_table):
    fp32, bf16, i32, u32 = mybir.dt.float32, mybir.dt.bfloat16, mybir.dt.int32, mybir.dt.uint32
    ACT = mybir.ActivationFunctionType
    ALU = mybir.AluOpType
    X = mybir.AxisListType.X
    ctx = ExitStack()
    with ctx:
        def sb(name, shape, dt=fp32):
            return ctx.enter_context(nc.sbuf_tensor(name, shape, dt))

        def sem(name):
            return ctx.enter_context(nc.semaphore(name))

        SLOT = 4096
        wts = sb("wts", [P, 6 * SLOT])
        w_in_sb = wts[:, 0:KT * IN_COLS].rearrange("p (k n) -> p k n", k=KT)
        w_out_sb = wts[:, 0:KT * D].rearrange("p (k n) -> p k n", k=KT)
        k_ring = wts[:, 5 * SLOT:6 * SLOT].rearrange("p (s g n) -> p s g n", s=RING, g=GP)
        v_ring = sb("v_ring", [P, RING, GP, AW])
        x_in = sb("x_in", [P, D])
        x2 = x_in
        h_tok = sb("h_tok", [P, D])
        h_T = sb("h_T", [P, KT, P])
        qk = sb("qk", [P, 2 * AW])
        rot = sb("rot", [P, 2 * AW])
        exps = [qk[:, 0:SEQ], qk[:, SEQ:2 * SEQ]]
        a_tok = rot[:, 0:SEQ]
        a_T = rot[:, SEQ:2 * SEQ]
        v_tok = sb("v_tok", [P, TILES, AW])
        u_tok = sb("u_tok", [P, CH])
        q_T = sb("q_T", [P, H, SEQ])
        k_T = sb("k_T", [P, H, SEQ])
        u_T = sb("u_T", [P, CT, TAPS - 1 + SEQ])
        mix = sb("mix", [P, 2 * H * TOK])
        mix_T = mix[:, :].rearrange("p (k n) -> p k n", k=2 * H)
        sext = mix[:, H * TOK:H * TOK + CT * NB * TAPS].rearrange("p (c b j) -> p c b j", c=CT, b=NB)
        norm_b = sb("norm_b", [P, D])
        q_b = sb("q_b", [P, 2, AW])
        v_new = sb("v_new", [1, AW])
        s_new = sb("s_new", [1, NB * HC])
        sc = sb("sc", [P, 2, PAGES + 1, HC])
        ex = sb("ex", [P, PAGES + 1, HC])
        e_pad = sb("e_pad", [P, H, 32])
        rope = sb("rope", [P, TILES + 1, 2, 32])
        wqk = sb("wqk", [P, 2, QD])
        cw = sb("cw", [P, 2, 2 * QD])
        conv_tmp = sb("conv_tmp", [P, CT * P])
        conv_tmpv = conv_tmp[:, :].rearrange("p (c n) -> p c n", c=CT)
        w_T = sb("w_T", [P, CT, TAPS])
        zs = sb("zs", [P, CT, NB])
        conv_w_in = k_T[0:TAPS, 0, :]
        lam4 = k_T[:, 1, 0:4 * QD].rearrange("p (i n) -> p i n", i=4)
        vecs = k_T[0:16, 2, 0:P]
        state_in = q_T[0:120, 0:2, :]
        vec_T = sb("vec_T", [P, 16])
        neg_gb = sb("neg_gb", [P, 2 * CT])
        sub_w = sb("sub_w", [P, 1])
        ident = sb("ident", [P, P])
        ones = sb("ones", [P, P])
        upper = sb("upper", [P, P])
        cmask = sb("cmask", [P, P])
        cmap = sb("cmap", [P, C, H])
        pad1 = sb("pad1", [P, 1])
        nlam = sb("nlam", [P, 1])
        eps_c = sb("eps_c", [P, 1])
        stl, stn, stp, stq, str_, sto = [sb(n, [P, w]) for n, w in (
            ("stl", 8), ("stn", 4), ("stp", 48), ("stq", 32), ("str_", 16), ("sto", 64))]
        snw = sb("snw", [P, HC])
        pmax = sb("pmax", [P, HC])
        mx = sb("mx", [HC, 1])
        dg = sb("dg", [HC, HC])
        rl = sb("rl", [P, 1])
        coef = sb("coef", [P, H])
        ot = sb("ot", [P, H * NB])
        ot_sq = sb("ot_sq", [P, H * NB])
        us = sb("us", [P, VD])
        ef = sb("ef", [1, TCOLS])
        iota_o = sb("iota_o", [P, OVF + 1])
        pages_sb = sb("pages_sb", [1, NB * PAGES], i32)
        route = q_T[:, 2:4, :].rearrange("p a n -> p (a n)")
        onehot = route[:, 0:640].rearrange("p (t k e) -> p t k e", t=TILES + 1, k=TOPK)
        chosen = route[:, 640:800].rearrange("p (t e) -> p t e", e=E)
        gtmp = route[:, 800:928].rearrange("p (k e) -> p k e", e=E)
        ad = route[:, 928:1008].rearrange("p (a n) -> p a n", a=4)
        r_w = k_T[:, 0, 0:KT * E].rearrange("p (k e) -> p k e", e=E)
        g_T = k_T[0:E, 0, 256:384]
        gsum = k_T[:, 0, 480:480 + E]
        cnt = k_T[:, 0, 384:480].rearrange("p (a e) -> p a e", e=E)
        r_b = sb("r_b", [P, E])
        iota_e = sb("iota_e", [P, E])
        logit = sb("logit", [P, E])
        top8 = sb("top8", [P, 8])
        idx8 = sb("idx8", [P, 8], u32)
        idxf = sb("idxf", [P, 8])
        gates = sb("gates", [P, TILES + 1, TOPK])
        rankk = sb("rankk", [P, TILES + 1, TOPK])
        PS = [ctx.enter_context(nc.psum_tensor(f"bank{i}", [P, 512], fp32)) for i in range(8)]
        A, T, U, O, M, S7 = PS[0:2], PS[2:4], PS[4], PS[5], PS[6], PS[7]

        bd = q_T[0:E, 0:2, :].rearrange("p a n -> p (a n)")
        g_act = q_T[:, 0, :]
        u_act = q_T[:, 1, :]
        s_act = q_T[:, 2, :]
        act_tok = q_T[:, 3, :]
        act_T = k_T[:, 0:2, :].rearrange("p a (b n) -> p (a b) n", n=P)
        y_sb = k_T[:, 2:4, :].rearrange("p a n -> p (a n)")
        xg = h_tok
        hg_T = h_T
        b_stage = mix[0:96, 0:2 * F]
        b_split = u_T[:, :, :].rearrange("p a n -> p (a n)")[:, 0:F].bitcast(bf16)
        sel = v_tok[:, 0, 0:P // 2].bitcast(bf16)
        pick3 = v_tok[:, 0, 64:64 + E // 2].bitcast(bf16)
        slots = v_tok[:, 1, 0:TCOLS].bitcast(i32)
        slot_tok = v_tok[:, 1, 64:64 + TCOLS].bitcast(i32)
        g_idx = v_tok[:, 1, 128:129].bitcast(i32)
        y_idx = v_tok[:, 1, 129:130].bitcast(i32)
        fill_i = v_tok[:, 1, 130:130 + TCOLS].bitcast(i32)
        e_tab = v_tok[0:1, 1, 192:192 + TCOLS].bitcast(i32)
        n_ovf = v_tok[0:1, 1, 250:251].bitcast(i32)
        addr = v_tok[:, 2, 0:20].bitcast(i32)
        pair_id = v_tok[:, 2, 32:52].bitcast(i32)
        tA = v_tok[:, 3, 0:64]
        tB = v_tok[:, 3, 64:128]
        tC = v_tok[:, 3, 128:192]
        big = y_sb[:, 0:(TILES + 1) * TOPK * E].rearrange("p (t e) -> p t e", e=E)
        out_rows = [wts[:, n * 8192:n * 8192 + 5 * D] for n in range(2)]

        ORDER = [("P", 0), ("C", 0)] + [(kind, s) for s in range(1, TILES + 1) for kind in "PQ"] + \
                [(kind, s) for s in range(1, TILES + 1) for kind in "LWR"] + \
                [("O", 0), ("L", 0), ("W", 0), ("R", 0)]
        USES = {"P": (5, 5, 1), "C": (0, 4, 0), "Q": (8, 5, 0), "L": (0, 0, 0), "W": (2, 0, 0), "R": (2, 2, 1),
                "O": (0, 0, 0)}
        TAIL = [1, 2, 3, 4, 0]
        base, a, t, h = {}, 0, 0, 0
        for part in ORDER:
            base[part] = (a, t, h)
            da, dt_, dh = USES[part[0]]
            if part == ("P", 0):
                dt_ = 3
            a, t, h = a + da, t + dt_, h + dh

        def rows_of(s):
            return NB if s == 0 else P

        def tail_no(s):
            return TAIL.index(s)

        x_rows = [x_sample[:, 0, :]] + [x_prompt[0, n * P:(n + 1) * P, :] for n in range(TILES)]
        row0 = [SEQ] + [n * P for n in range(TILES)]
        v_rows = [conv_tmp[0:NB, :]] + [v_tok[:, n, :] for n in range(TILES)]
        kc = cache_k[0].rearrange("n p h c d -> n p (h c d)")
        vc = cache_v[0].rearrange("n p h d -> n p (h d)")
        new_k_rows = [new_k_s[0, :, 0].rearrange("b h c d -> b (h c d)")] + \
                     [new_k_p[0, 0, n * P:(n + 1) * P].rearrange("b h c d -> b (h c d)") for n in range(TILES)]
        new_v_rows = [new_v_s[0, :, 0].rearrange("b h d -> b (h d)")] + \
                     [new_v_p[0, 0, n * P:(n + 1) * P].rearrange("b h d -> b (h d)") for n in range(TILES)]
        y_out = [y_sample[:, 0, :]] + [y_prompt[0, n * P:(n + 1) * P, :] for n in range(TILES)]

        a_full, a_free = [sem(f"a_full{n}") for n in range(2)], [sem(f"a_free{n}") for n in range(2)]
        t_full, t_free = [sem(f"t_full{n}") for n in range(2)], [sem(f"t_free{n}") for n in range(2)]
        k_full = [sem(f"k_full{n}") for n in range(RING)]
        v_full = [sem(f"v_full{n}") for n in range(RING)]
        w_full = [sem(f"w_full{n}") for n in range(6)]
        w_used = [sem(f"w_used{n}") for n in range(6)]
        y_loaded = [sem(f"y_loaded{n}") for n in range(2)]
        y_stored = [sem(f"y_stored{n}") for n in range(2)]
        (setup_in, x_loaded, norm1_in, win_in, wout_in, xw_loaded, norm2_in, sample_rows_out, pages_in,
         lam_in) = [sem(n) for n in ("setup_in", "x_loaded", "norm1_in", "win_in", "wout_in", "xw_loaded",
                                     "norm2_in", "sample_rows_out", "pages_in", "lam_in")]
        (pool_consts, rstd_done, h_done, qk_copied, v_copied, eb_done, u_done, ss16_done, r16_done, rot_done,
         k_out, v_out, u_out, state_out, conv_done, sample_conv_done, vecs_done) = [sem(n) for n in (
             "pool_consts", "rstd_done", "h_done", "qk_copied", "v_copied", "eb_done", "u_done", "ss16_done",
             "r16_done", "rot_done", "k_out", "v_out", "u_out", "state_out", "conv_done", "sample_conv_done", "vecs_done")]
        (kmul_done, kred_done, pm_done, small_pe, gm_ready, sub_done, exp_done, es_done, pv_done, u_all,
         coef_done, us_done, qb_in, vn_in, sn_in, cmap_done) = [sem(n) for n in (
             "kmul_done", "kred_done", "pm_done", "small_pe", "gm_ready", "sub_done", "exp_done", "es_done",
             "pv_done", "u_all", "coef_done", "us_done", "qb_in", "vn_in", "sn_in", "cmap_done")]
        (max_done, pexp_done, comb_done, o_full, osq_done, oss_done, or_done, on_done) = [sem(n) for n in (
            "max_done", "pexp_done", "comb_done", "o_full", "osq_done", "oss_done", "or_done", "on_done")]
        (mean_done, zc_done, zsq_done, var_done, vr_done, zn_done, ez_done, mix_done, x2_done, h2_out,
         logits_done, logit_read, gexp_done, gexp_ask, gate_done, rank_done, rank_read, gT_done, gT_copied,
         bd_in, rw_in, x2_out) = [sem(n) for n in (
             "mean_done", "zc_done", "zsq_done", "var_done", "vr_done", "zn_done", "ez_done", "mix_done",
             "x2_done", "h2_out", "logits_done", "logit_read", "gexp_done", "gexp_ask", "gate_done",
             "rank_done", "rank_read", "gT_done", "gT_copied", "bd_in", "rw_in", "x2_out")]
        (ot_done, otsq_done, otss_done, otr_done) = [sem(n) for n in ("ot_done", "otsq_done", "otss_done",
                                                                      "otr_done")]
        (counts_done, addr_done, table_zeroed, table_written, table_in, meta_out, meta_in, bias_in,
         bias_split, fill_done, idx_done, gathered, y_scattered, pair_done) = [sem(n) for n in (
             "counts_done", "addr_done", "table_zeroed", "table_written", "table_in", "meta_out", "meta_in",
             "bias_in", "bias_split", "fill_done", "idx_done", "gathered", "y_scattered", "pair_done")]
        (xt_full, xt_copied, gu_full, gclip_done, sig_done, act_done, at_full, at_copied, y_full, y_copied,
         sel_done) = [sem(n) for n in ("xt_full", "xt_copied", "gu_full", "gclip_done", "sig_done",
                                       "act_done", "at_full", "at_copied", "y_full", "y_copied", "sel_done")]
        act_step, dve_step, pool_step, dve_loop_step = [sem(n) for n in ("act_step", "dve_step", "pool_step",
                                                                         "dve_loop_step")]
        block = ctx.enter_context(nc.Block())

        def after(eng, s, value):
            if isinstance(value, int) and value <= 0:
                return
            eng.wait_ge(s, value)

        def t_view(bank, n):
            return bank[:, :].rearrange("p (i n) -> p i n", n=P)[:, :, 0:n]

        H_PARTS = [p for p in ORDER if USES[p[0]][2]]

        def after_h_tok_read(eng, part):
            no = base[part][2]
            if no:
                k = base[H_PARTS[no - 1]][1] + 1
                eng.wait_ge(t_full[k % 2], k // 2 + 1)
                if H_PARTS[no - 1][0] == "R":
                    eng.wait_ge(h2_out, 16 * (tail_no(H_PARTS[no - 1][1]) + 1))

        def after_h_T_read(eng, part):
            no = base[part][2]
            if no:
                kind, s = H_PARTS[no - 1]
                if kind == "P":
                    k = base[(kind, s)][0] + 4
                    eng.wait_ge(a_full[k % 2], k // 2 + 1)
                else:
                    eng.wait_ge(logits_done, tail_no(s) + 1)

        def filled(full, k):
            return full[k % 2], k // 2 + 1

        SLOTS_OF_STEP = [2 if g % 4 == 3 else 1 for g in range(NG)]
        V_OF_STEP = {3: (0, 1), 4: (2, 3), 5: (4, 5), **{g: (g,) for g in range(6, NG)}}

        def run_with_samples(step, mixer):
            for b in range(-1, NB):
                for g in range(NG):
                    step(b, g)
                    for _ in range(SLOTS_OF_STEP[g]):
                        next(mixer, None)
            for _ in mixer:
                pass

        w_slot = [wts[:, n * SLOT:(n + 1) * SLOT] for n in range(6)]
        CHUNK_SLOT = [2, 3, 4, 5, 0, 1]
        gu_chunk = [w_slot[CHUNK_SLOT[c]].rearrange("p (k g n) -> p k g n", k=4, g=2) for c in range(4)]
        dn_chunk = [w_slot[CHUNK_SLOT[4 + c]].rearrange("p (k n) -> p k n", k=4) for c in range(2)]

        @block.sync
        def _(sp):
            sp.dma_start(x_in[0:NB, :], x_rows[0]).then_inc(x_loaded, 16)
            sp.dma_start(norm_b[:, :], norm1_w[0].partition_broadcast(P)).then_inc(norm1_in, 16)
            for k in range(KT):
                sp.dma_start(w_in_sb[:, k, :], w_in[0, k * P:(k + 1) * P, :]).then_inc(win_in, 16)
            sp.wait_ge(pages_in, 16)

            def load_pages(ring, full, cache, used, first_page, r, need):
                if need is not None:
                    sp.wait_ge(used, need)
                for p in range(GP):
                    page = sp.value_load(pages_sb[0:1, bass.ds(first_page + p, 1)],
                                         min_val=0, max_val=cache.shape[0] - 1)
                    sp.dma_start(ring[:, r, p, :],
                                 cache[bass.ds(page, 1)].rearrange("a p n -> (a p) n")).then_inc(full[r], 16)

            def load_q(b, even):
                sp.dma_start(q_b[:, 0 if even else 1, :],
                             q_rows[bass.ds(b, 1), :].rearrange("a n -> (a n)").partition_broadcast(P)
                             ).then_inc(qb_in, 16)

            def load_k(b, four, r, first=False):
                g = four * RING + r
                load_pages(k_ring, k_full, kc, kred_done, b * PAGES + g * GP, r,
                           None if first else b * NG + (g + 1 - RING))

            def load_v(b, four, r, first=False):
                g = four * RING + r
                load_pages(v_ring, v_full, vc, pv_done, b * PAGES + g * GP, r,
                           None if first else b * NG + (g + 1 - RING))

            def step(b, first=False, last=False):
                for half in range(2):
                    if first and half == 0:
                        for r in range(RING):
                            load_k(b + 1, 0, r)
                            load_v(b, 0, r, True)
                    with sp.Fori(1 if first and half == 0 else 2 * half, 2 * half + 2) as four:
                        for r in range(RING):
                            if not last:
                                load_k(b + 1, four, r)
                            load_v(b, four, r)
                    if half == 0:
                        if not first:
                            sp.wait_ge(u_all, b)
                        sp.dma_start(v_new[0:1, :], new_v_rows[0][bass.ds(b, 1), :]).then_inc(vn_in, 16)

            sp.wait_ge(sample_rows_out, 64)
            load_q(0, True)
            load_q(1, False)
            for r in range(RING):
                load_k(0, 0, r, True)
            with sp.Fori(1, NG // RING) as four:
                for r in range(RING):
                    load_k(0, four, r)
            step(0, first=True)
            with sp.Fori(0, (NB - 2) // 2) as pair:
                b = pair * 2 + 1
                for odd in range(2):
                    sp.wait_ge(kred_done, b * NG + odd * NG)
                    load_q(b + (odd + 1), odd == 0)
                    step(b + odd)
            step(NB - 1, last=True)

            def load_chunk(c, e):
                if c < 4:
                    half, kq = c // 2, c % 2
                    for part in range(2):
                        n0 = part * F + half * 512
                        src = w_gate_up[0][bass.ds(e, 1), kq * 512:(kq + 1) * 512, n0:n0 + 512].rearrange(
                            "a (k p) n -> (a p) k n", p=P)
                        sp.dma_start(gu_chunk[c][:, :, part, :], src).then_inc(w_full[c], 16)
                else:
                    q = c - 4
                    src = w_down[0][bass.ds(e, 1), q * 512:(q + 1) * 512, :].rearrange(
                        "a (k p) n -> (a p) k n", p=P)
                    sp.dma_start(dn_chunk[q], src).then_inc(w_full[c], 16)

            k, n = filled(a_full, base[("P", TILES)][0] + 4)
            sp.wait_ge(k, n)
            for c in range(3):
                load_chunk(c, 0)
            sp.wait_ge(kred_done, NB * NG)
            load_chunk(3, 0)
            k, n = filled(a_full, base[("W", 0)][0] + 1)
            sp.wait_ge(k, n)
            for c in range(4, 6):
                load_chunk(c, 0)
            with sp.Fori(1, E) as i:
                for c in range(6):
                    sp.wait_ge(w_used[c], i)
                    load_chunk(c, i)
            sp.wait_ge(meta_out, 1)
            n = sp.value_load(n_ovf[0:1, 0:1], min_val=0, max_val=OVF)
            with sp.Fori(0, OVF) as j:
                with sp.If(j < n):
                    e = sp.value_load(e_tab[0:1, bass.ds(j + E, 1)], min_val=0, max_val=E - 1)
                    for c in range(6):
                        sp.wait_ge(w_used[c], j + E)
                        load_chunk(c, e)

            sp.wait_ge(y_scattered, (n + E) * 16)
            sp.wait_ge(w_used[5], n + E)
            sp.wait_ge(x2_out, 16 * (TILES + 1))
            for u, s in enumerate(TAIL):
                m, b = rows_of(s), u % 2
                if u >= 2:
                    sp.wait_ge(y_stored[b], 16 * (u // 2))
                r = row0[s]
                sp.dma_start(out_rows[b][0:m, 0:TOPK * D],
                             y_rows[r * TOPK:(r + m) * TOPK, :].rearrange("(p k) n -> p (k n)", k=TOPK)
                             ).then_inc(y_loaded[b], 16)
                sp.dma_start(out_rows[b][0:m, TOPK * D:], x2_rows[r:r + m, :]).then_inc(y_loaded[b], 16)
            for u, s in enumerate(TAIL):
                m, b = rows_of(s), u % 2
                sp.wait_ge(y_stored[b], 16 * (u // 2 + 1))

        @block.gpsimd
        def _(pool):
            V = Chain(pool, pool_step)
            V.link(nc.gpsimd.memset(ident[:, :], 0.0))
            V.link(pool.affine_select(out=ident[:, :], in_=ident[:, :], compare_op=ALU.not_equal, fill=1.0,
                                      base=0, pattern=[[-1, P]], channel_multiplier=1))
            V.link(nc.gpsimd.memset(ones[:, :], 1.0))
            V.link(pool.affine_select(out=upper[:, :], in_=ones[:, :], compare_op=ALU.is_gt, fill=0.0,
                                      base=0, pattern=[[1, P]], channel_multiplier=-1))
            V.link(nc.gpsimd.memset(cmask[:, :], 0.0))
            V.link(pool.affine_select(out=cmask[:, :], in_=cmask[:, :], compare_op=ALU.is_ge, fill=NEG,
                                      base=0, pattern=[[-1, P]], channel_multiplier=1))
            V.link(nc.gpsimd.memset(eps_c[:, :], EPS))
            V.link(nc.gpsimd.memset(u_T[:, :, 0:TAPS - 1], 0.0))
            V.link(nc.gpsimd.memset(sc[:, :, PAGES, :], NEG))
            V.link(nc.gpsimd.memset(e_pad[:, :, :], 0.0))
            V.link(pool.iota(iota_e[:, :], [[1, E]], base=0, channel_multiplier=0,
                             allow_small_or_imprecise_dtypes=True))
            V.link(nc.gpsimd.memset(cmap[:, :, :], 0.0))
            for c in range(C):
                V.link(pool.affine_select(out=cmap[:, c, :], in_=cmap[:, c, :], compare_op=ALU.not_equal,
                                          fill=1.0, base=-c, pattern=[[-32, H]], channel_multiplier=1))
            pool.iota(iota_o[:, :], [[1, OVF + 1]], base=0, channel_multiplier=0,
                      allow_small_or_imprecise_dtypes=True).then_inc(pool_consts, 1)

            for s in range(1, TILES + 1):
                k, n = filled(t_free, base[("P", s)][1] + 4)
                pool.wait_ge(k, n)
                if s == 1:
                    pool.wait_ge(sample_conv_done, 1)
                    pool.wait_ge(sample_rows_out, 64)
                r = row0[s]
                z = mix_T[:, H:2 * H, r:r + P]
                for ct in range(CT):
                    V.link(nc.gpsimd.tensor_scalar(z[:, ct, :], u_T[:, ct, r:r + P], w_T[:, ct, 0:1],
                                                   vec_T[:, ct:ct + 1], ALU.mult, ALU.add))
                for j in range(1, TAPS):
                    w = w_T[:, :, j:j + 1].to_broadcast([P, CT, P])
                    V.link(nc.gpsimd.tensor_tensor(conv_tmpv, u_T[:, :, r + j:r + j + P], w, ALU.mult))
                    last = nc.gpsimd.tensor_tensor(z, z, conv_tmpv, ALU.add)
                    if j < TAPS - 1:
                        V.link(last)
                last.then_inc(conv_done, 1)
                pool.wait_ge(conv_done, s)

            k, n = filled(t_full, base[("Q", TILES)][1] + 4)
            pool.wait_ge(k, n)
            pool.wait_ge(v_out, 16 * TILES)
            V.link(pool.iota(fill_i, [[0, TCOLS]], base=UNUSED, channel_multiplier=TOPK))
            pool.dma_start(slot_table.rearrange("(p c) o -> p (c o)", c=TCOLS), fill_i).then_inc(table_zeroed, 16)
            V.link(pool.iota(pair_id.rearrange("p (t k) -> p t k", k=TOPK), [[TOPK * P, TILES + 1], [1, TOPK]],
                             base=0, channel_multiplier=TOPK))
            pool.wait_ge(table_zeroed, 16)
            pool.wait_ge(addr_done, 1)
            for u, s in enumerate(TAIL):
                m = rows_of(s)
                for kk in range(TOPK):
                    col = u * TOPK + kk
                    pool.indirect_dma_start(slot_table[:, :], bass.IndirectOffsetOnAxis(addr[0:m, col:col + 1], 0),
                                            pair_id[0:m, col:col + 1], None).then_inc(table_written, 16)
            pool.wait_ge(table_written, 16 * (TILES + 1) * TOPK)
            pool.dma_start(slots, slot_table.rearrange("(p c) o -> p (c o)", c=TCOLS)).then_inc(table_in, 16)

            bound, rows_0 = pool.alloc_register("bound"), pool.alloc_register("rows_0")
            pool.reg_mov(rows_0, 0)

            def gather(i, first):
                if not first:
                    pool.wait_ge(xt_full, i * 2)
                pool.wait_ge(idx_done, 1)
                V.link(nc.gpsimd.tensor_copy(g_idx, slot_tok[:, bass.ds(i, 1)]))
                pool.reg_add(bound, rows_0, TOK - 1)
                pool.indirect_dma_start(xg[:, :], None, h2_rows[:, :], bass.IndirectOffsetOnAxis(g_idx, 0),
                                        bounds_check=bound, oob_is_err=False).then_inc(gathered, 16)

            def scatter(i, first):
                pool.wait_ge(y_copied, i + 1)
                if not first:
                    pool.wait_ge(y_scattered, i * 16)
                pool.wait_ge(table_in, 16)
                V.link(nc.gpsimd.tensor_copy(y_idx, slots[:, bass.ds(i, 1)]))
                pool.reg_add(bound, rows_0, PAIRS - 1)
                pool.indirect_dma_start(y_rows[:, :], bass.IndirectOffsetOnAxis(y_idx, 0), y_sb, None,
                                        bounds_check=bound, oob_is_err=False).then_inc(y_scattered, 16)

            pool.wait_ge(idx_done, 1)
            pool.wait_ge(h2_out, 16 * (TILES + 1))
            k, n = filled(t_full, base[("R", 0)][1] + 1)
            pool.wait_ge(k, n)
            gather(0, True)
            V.base, V.n = V.n, 0
            gather(1, False)
            scatter(0, True)
            start = V.base + V.n
            with pool.Fori(1, E) as i:
                V.base, V.n = i * 2 + (start - 2), 0
                gather(i + 1, False)
                scatter(i, False)
            pool.wait_ge(meta_out, 1)
            n = pool.value_load(n_ovf[0:1, 0:1], min_val=0, max_val=OVF)
            with pool.Fori(0, OVF) as j:
                with pool.If(j < n):
                    V.base, V.n = j * 2 + (start + 2 * (E - 1)), 0
                    gather(j + (E + 1), False)
                    scatter(j + E, False)

        @block.scalar
        def _(act):
            V = Chain(act, act_step)
            act.dma_start(pages_sb[:, :], page_table.rearrange("b n -> (b n)").rearrange("(a n) -> a n", a=1)
                          ).then_inc(pages_in, 16)
            for i, vec in enumerate((lambda_q1, lambda_k1, lambda_q2, lambda_k2)):
                act.dma_start(lam4[:, i, :], vec[0].partition_broadcast(P)).then_inc(lam_in, 16)
            n_in = [0]

            def small(dst, src):
                n_in[0] += 16
                act.dma_start(dst, src).then_inc(setup_in, 16)

            small(vecs[0:4, :], conv_b[0].rearrange("(c p) -> c p", p=P))
            small(vecs[4:8, :], conv_ln_g[0].rearrange("(c p) -> c p", p=P))
            small(vecs[8:12, :], conv_ln_b[0].rearrange("(c p) -> c p", p=P))
            small(vecs[12:13, :], subln_w)
            small(conv_w_in, conv_w[0])
            small(state_in,
                  state_conv[0].rearrange("(r b) j c -> (b j) r c", r=2))
            small(rope[:, 1:, :, :], rope_table[0:SEQ].rearrange("(t p) a n -> p t a n", p=P))
            small(rope[0:NB, 0, :, :], rope_table[SEQ:TOK])
            small(wqk[:, 0, :], q_norm_w[0].partition_broadcast(P))
            small(wqk[:, 1, :], k_norm_w[0].partition_broadcast(P))
            small(r_b[:, :], router_b[0].partition_broadcast(P))
            act.dma_start(new_conv_s[0, :, 0:TAPS - 2, :], state_conv[0, :, 1:TAPS - 1, :]).then_inc(state_out, 16)
            act.preload_act_table_set("natural_log_exp_and_others")
            act.wait_ge(pool_consts, 1)
            act.wait_ge(ss16_done, 1)
            nc.scalar.activation(stl[:, 4:6], stl[:, 2:4], ACT.Exp).then_inc(r16_done, 1)

            def rstd(out, tmp, ss, scale, signal):
                V.link(nc.scalar.activation(tmp, ss, ACT.Ln, bias=eps_c[0:ss.shape[0], :], scale=scale))
                nc.scalar.activation(out, tmp, ACT.Exp, scale=-0.5).then_inc(signal, 1)

            def normalise(part, src, n):
                after_h_tok_read(act, part)
                V.link(nc.scalar.activation(h_tok[0:n, :], src[0:n, :], ACT.Square, accum_out=stn[0:n, 0:1]))
                rstd(stn[0:n, 2:3], stn[0:n, 1:2], stn[0:n, 0:1], 1.0 / D, rstd_done)

            def copy_t(k, dst, src, scale=1.0):
                act.wait_ge(*filled(t_full, k))
                nc.scalar.activation(dst, src, ACT.Copy, scale=scale).then_inc(t_free[k % 2], 1)

            def copy_h(part, n):
                t0 = base[part][1]
                after_h_T_read(act, part)
                for q in range(2):
                    copy_t(t0 + q, h_T[:, 4 * q:4 * q + 4, 0:n], t_view(T[(t0 + q) % 2], n))

            def part_p(s):
                n, (a0, t0, _h) = rows_of(s), base[("P", s)]
                act.wait_ge(x_loaded, 16 * (s + 1))
                normalise(("P", s), x_in, n)
                yield
                act.wait_ge(h_done, base[("P", s)][2] + 1)
                if s < TILES:
                    act.dma_start(x_in[:, :], x_rows[s + 1]).then_inc(x_loaded, 16)
                else:
                    act.dma_start(norm_b[:, :], norm2_w[0].partition_broadcast(P)).then_inc(norm2_in, 16)
                copy_h(("P", s), n)
                yield
                for c in range(5):
                    yield
                    k = a0 + c
                    if c != 3:
                        act.wait_ge(*filled(a_full, k))
                    if c < 2:
                        after(act, rot_done, s)
                        after(act, comb_done, H * (s - 1))
                        nc.scalar.activation(qk[0:n, c * 512:(c + 1) * 512], A[k % 2][0:n, :], ACT.Copy
                                             ).then_inc(a_free[k % 2], 1)
                    elif c == 2:
                        nc.scalar.activation(v_rows[s], A[k % 2][0:n, :], ACT.Copy
                                             ).then_inc(a_free[k % 2], 1)
                        act.wait_ge(ss16_done, s + 2)
                        rstd(stp[0:n, 32:48], stp[0:n, 16:32], stp[0:n, 0:16], 1.0 / QD, r16_done)
                    elif c == 4:
                        if s:
                            act.wait_ge(*filled(t_full, base[("P", s - 1)][1] + (4 if s > 1 else 2)))
                            act.wait_ge(u_out, 16)
                        nc.scalar.activation(u_tok[0:n, :], A[k % 2][0:n, :], ACT.Exp, scale=-1.0
                                             ).then_inc(a_free[k % 2], 1)
                    yield
                act.wait_ge(rot_done, s + 1)
                act.dma_start(new_k_rows[s], rot[0:n, AW:]).then_inc(k_out if s else sample_rows_out, 16)
                act.wait_ge(*filled(a_free, a0 + 2))
                act.dma_start(new_v_rows[s], v_rows[s]).then_inc(v_out if s else sample_rows_out, 16)
                if s:
                    cols = slice(row0[s], row0[s] + P)
                    copy_t(t0 + 2, q_T[:, :, cols], t_view(T[(t0 + 2) % 2], P))
                    copy_t(t0 + 3, k_T[:, :, cols], t_view(T[(t0 + 3) % 2], P))
                else:
                    act.dma_start(q_rows[:, :], rot[0:n, 0:AW]).then_inc(sample_rows_out, 16)
                    act.wait_ge(kmul_done, 1)
                    act.dma_start(s_new_rows[:, :], snw[0:n, :]).then_inc(sample_rows_out, 16)
                yield
                act.wait_ge(*filled(a_free, a0 + 3))
                if s == 0:
                    act.dma_start(new_conv_s[0, :, TAPS - 2, :], u_tok[0:n, :]).then_inc(u_out, 16)
                if s == TILES:
                    act.dma_start(new_conv_p[0, 0], u_tok[P - (TAPS - 1):P, :]).then_inc(u_out, 16)
                if s:
                    k = t0 + 4
                    copy_t(k, u_T[:, :, TAPS - 1 + row0[s]:TAPS - 1 + row0[s] + P], t_view(T[k % 2], P))
                else:
                    k = t0 + 2
                    copy_t(k, sext[:, :, :, TAPS - 1], t_view(T[k % 2], NB))
                    act.wait_ge(sample_rows_out, 64)
                    act.dma_start(s_new[:, :], s_new_rows.rearrange("b n -> (b n)").rearrange(
                        "(a n) -> a n", a=1)).then_inc(sn_in, 16)
                yield

            def part_c():
                t0 = base[("C", 0)][1]
                copy_t(t0, vec_T[:, 0:13], T[t0 % 2][:, 0:13])
                copy_t(t0 + 1, w_T[:, :, :], T[(t0 + 1) % 2][:, 0:CT * TAPS].rearrange("p (c j) -> p c j", c=CT))
                for r in range(2):
                    k = t0 + 2 + r
                    src = T[k % 2][:, 0:480].rearrange("p (c b j) -> p c b j", c=CT, b=4)
                    act.wait_ge(*filled(t_full, k))
                    for ct in range(CT):
                        ins = nc.scalar.activation(sext[:, ct, 4 * r:4 * r + 4, 0:TAPS - 1], src[:, ct], ACT.Copy)
                        if ct < CT - 1:
                            V.link(ins)
                    ins.then_inc(t_free[k % 2], 1)

            def part_q(s):
                t, (a0, t0, _h) = s - 1, base[("Q", s)]
                kw = (t + 1) * P
                for h in range(H):
                    yield
                    act.wait_ge(max_done, H * t + h + 1)
                    after(act, comb_done, H * t + h)
                    for c in range(C):
                        b = (a0 + 2 * h + c) % 2
                        nc.scalar.activation(exps[c][:, 0:kw], A[b][:, 0:kw], ACT.Exp, bias=stq[:, 2 + c:3 + c],
                                             scale=SM_SCALE, accum_out=stq[:, 4 + c:5 + c]
                                             ).then_inc(a_free[b], 1)
                    yield
                    k = t0 + h
                    after(act, o_full, H * t + h)
                    copy_t(k, a_T[:, 0:kw], T[k % 2][:, 0:kw])
                    yield
                act.wait_ge(o_full, H * (t + 1))
                act.wait_ge(*filled(t_full, t0 + H - 1))
                nc.scalar.activation(a_tok, O[:, :], ACT.Square).then_inc(osq_done, 1)
                yield
                act.wait_ge(oss_done, t + 1)
                rstd(stq[:, 16:20], stq[:, 12:16], stq[:, 8:12], 1.0 / VD, or_done)
                yield
                k = t0 + H
                copy_t(k, mix_T[:, 0:H, row0[s]:row0[s] + P], t_view(T[k % 2], P), scale=sub_w[:, :])
                yield

            ln_sq = [exps[0][:, :].rearrange("p (c n) -> p c n", c=CT), exps[1]]

            def part_l(s):
                u, n, r = tail_no(s), rows_of(s), row0[s]
                z = mix_T[:, H:2 * H, r:r + n]
                if u:
                    act.wait_ge(x2_out, 16 * u)
                act.dma_start(x2[0:n, :], x_rows[s]).then_inc(xw_loaded, 16)
                if u == 0:
                    act.dma_start(w_out_sb, w_out[0].rearrange("(k p) n -> p k n", p=P)).then_inc(wout_in, 16)
                    act.dma_start(bd, b_down[0]).then_inc(bd_in, 16)
                    act.dma_start(r_w, router_w[0].rearrange("(k p) n -> p k n", p=P)).then_inc(rw_in, 16)
                yield
                act.wait_ge(zc_done, u + 1)
                nc.scalar.activation(ln_sq[0][:, :, 0:n], z, ACT.Square).then_inc(zsq_done, 1)
                yield
                act.wait_ge(var_done, u + 1)
                rstd(ln_sq[1][:, P:P + n], ln_sq[1][:, 0:n], M[:, P:P + n], 1.0 / CH, vr_done)
                yield
                act.wait_ge(zn_done, u + 1)
                for ct in range(CT):
                    ins = nc.scalar.activation(ln_sq[0][:, ct, 0:n], z[:, ct, :], ACT.Exp,
                                               scale=neg_gb[:, ct:ct + 1], bias=neg_gb[:, CT + ct:CT + ct + 1])
                    if ct < CT - 1:
                        V.link(ins)
                ins.then_inc(ez_done, 1)
                yield

            def part_w(s):
                yield from [None] * 4

            def part_r(s):
                u, n, r, (a0, t0, hn) = tail_no(s), rows_of(s), row0[s], base[("R", s)]
                for c in range(2):
                    act.wait_ge(*filled(a_free, base[("W", s)][0] + c))
                normalise(("R", s), x2, n)
                yield
                act.wait_ge(h_done, hn + 1)
                act.dma_start(h2_rows[r:r + n, :], h_tok[0:n, :]).then_inc(h2_out, 16)
                copy_h(("R", s), n)
                yield
                yield
                act.wait_ge(gexp_ask, u + 1)
                nc.scalar.activation(str_[0:n, 4:8], top8[0:n, 0:TOPK], ACT.Exp, bias=str_[0:n, 0:1],
                                     accum_out=str_[0:n, 1:2]).then_inc(gexp_done, 1)
                yield
                yield
                for c in range(2):
                    act.wait_ge(*filled(a_free, a0 + c))
                act.dma_start(x2_rows[r:r + n, :], x2[0:n, :]).then_inc(x2_out, 16)
                yield

            def sample_step(b, g):
                if b >= 0 and g == 2:
                    act.wait_ge(sub_done, b + 1)
                    after(act, u_all, b)
                    after(act, es_done, b)
                    nc.scalar.activation(ex[:, :, :], sc[:, b % 2, :, :], ACT.Exp, scale=SM_SCALE
                                         ).then_inc(exp_done, 1)

            for _ in part_p(0):
                pass
            part_c()
            parts = {"P": part_p, "Q": part_q, "L": part_l, "W": part_w, "R": part_r}
            run_with_samples(sample_step, (x for kind, s in ORDER[2:-4] for x in parts[kind](s)))
            act.wait_ge(otsq_done, 1)
            rstd(sto[:, 0:32], sto[:, 32:64], M[:, 448:480], 1.0 / VD, otr_done)
            for kind, s in ORDER[-3:]:
                for _ in parts[kind](s):
                    pass

            k, v = filled(a_full, base[("W", 0)][0] + 1)
            act.wait_ge(k, v)
            for q in range(3):
                act.dma_start(b_stage[32 * q:32 * q + 32, :], b_gate_up[0]).then_inc(bias_in, 16)

            act.preload_act_table_set("sigmoid_and_others")
            XB = [PS[6], PS[2]]
            AB = [PS[6], PS[7]]

            def copy_x(i, q):
                act.wait_ge(xt_full, i * 2 + (q + 1))
                nc.scalar.activation(hg_T[:, 4 * q:4 * q + 4, :], t_view(XB[q], P), ACT.Copy
                                     ).then_inc(xt_copied, 1)

            def expert_block(i):
                for half in range(2):
                    act.wait_ge(gclip_done, i * 2 + (half + 1))
                    after(act, act_done, i * 2 + half)
                    nc.scalar.activation(s_act, g_act, ACT.Sigmoid, scale=ALPHA).then_inc(sig_done, 1)
                    act.wait_ge(at_full, i * 2 + (half + 1))
                    if half == 0:
                        after(act, w_used[5], i)
                    nc.scalar.activation(act_T[:, 4 * half:4 * half + 4, :], t_view(AB[half], P), ACT.Copy
                                         ).then_inc(at_copied, 1)
                act.wait_ge(w_used[3], i + 1)
                for q in range(2):
                    copy_x(i + 1, q)

            for q in range(2):
                copy_x(0, q)
            expert_block(0)
            with act.Fori(1, E) as i:
                expert_block(i)
            act.wait_ge(meta_out, 1)
            n = act.value_load(n_ovf[0:1, 0:1], min_val=0, max_val=OVF)
            with act.Fori(0, OVF) as j:
                with act.If(j < n):
                    expert_block(j + E)
            for s, n in ((k_out, TILES), (v_out, TILES), (u_out, 2), (state_out, 1)):
                act.wait_ge(s, 16 * n)
            for u, s in enumerate(TAIL):
                m, b = rows_of(s), u % 2
                act.wait_ge(pair_done, TOPK * (u + 1))
                act.dma_start(y_out[s], out_rows[b][0:m, TOPK * D:]).then_inc(y_stored[b], 16)

        @block.tensor
        def _(pe):
            def fill_a(k):
                after(pe, a_free[k % 2], k // 2)

            def fill_t(k):
                after(pe, t_free[k % 2], k // 2)

            def transposes(k, src, n, count, cols=P):
                fill_t(k)
                for i in range(count):
                    m = pe.transpose(T[k % 2][0:cols, i * P:i * P + n], src[0:n, i * cols:(i + 1) * cols],
                                     ident[0:n, 0:n])
                m.then_inc(t_full[k % 2], 1)

            def transpose_h(part, n):
                t0, hn = base[part][1], base[part][2]
                pe.wait_ge(h_done, hn + 1)
                for q in range(2):
                    transposes(t0 + q, h_tok[:, 4 * q * P:(4 * q + 4) * P], n, 4)

            def part_p(s):
                n, (a0, t0, _h) = rows_of(s), base[("P", s)]
                yield
                transpose_h(("P", s), n)
                yield
                if s == 0:
                    pe.wait_ge(win_in, 16 * KT)
                for q in range(2):
                    pe.wait_ge(t_free[(t0 + q) % 2], (t0 + q) // 2 + 1)
                for c in range(5):
                    k = a0 + c
                    fill_a(k)
                    for kt in range(KT):
                        m = nc.tensor.matmul(A[k % 2][0:n, :], h_T[:, kt, 0:n],
                                             w_in_sb[:, kt, c * 512:(c + 1) * 512],
                                             start=(kt == 0), stop=(kt == KT - 1))
                        if kt == KT - 1:
                            m.then_inc(a_full[k % 2], 1)
                        if kt % 4 == 3:
                            yield
                if s:
                    pe.wait_ge(rot_done, s + 1)
                    transposes(t0 + 2, rot[:, 0:AW], P, 4)
                    transposes(t0 + 3, rot[:, AW:], P, 4)
                yield
                k, v = filled(a_free, a0 + 3)
                pe.wait_ge(k, v)
                transposes(t0 + (4 if s else 2), u_tok, n, 4)
                yield

            def part_c():
                t0 = base[("C", 0)][1]
                pe.wait_ge(setup_in, 16 * 11)
                fill_t(t0)
                pe.transpose(T[t0 % 2][:, 0:13], vecs[0:13, :], ident[0:13, 0:13]).then_inc(t_full[t0 % 2], 1)
                k = t0 + 1
                fill_t(k)
                for ct in range(CT):
                    m = pe.transpose(T[k % 2][:, ct * TAPS:(ct + 1) * TAPS], conv_w_in[:, ct * P:(ct + 1) * P],
                                     ident[0:TAPS, 0:TAPS])
                m.then_inc(t_full[k % 2], 1)
                for r in range(2):
                    k = t0 + 2 + r
                    fill_t(k)
                    for ct in range(CT):
                        m = pe.transpose(T[k % 2][:, ct * 120:(ct + 1) * 120],
                                         state_in[:, r, ct * P:(ct + 1) * P], ident[0:120, 0:120])
                    m.then_inc(t_full[k % 2], 1)

            def values(s, h):
                t = s - 1
                k = base[("Q", s)][1] + h
                pe.wait_ge(t_free[k % 2], k // 2 + 1)
                if h == 0:
                    after(pe, on_done, t)
                for kb in range(t + 1):
                    m = nc.tensor.matmul(O[:, h * VD:(h + 1) * VD], a_T[:, kb * P:(kb + 1) * P],
                                         v_tok[:, kb, h * VD:(h + 1) * VD], start=(kb == 0), stop=(kb == t))
                m.then_inc(o_full, 1)

            def part_q(s):
                t, (a0, t0, _h) = s - 1, base[("Q", s)]
                kw = (t + 1) * P
                pe.wait_ge(*filled(t_free, base[("P", s)][1] + 2))
                pe.wait_ge(*filled(t_free, base[("P", s)][1] + 3))
                for h in range(H):
                    if h:
                        values(s, h - 1)
                    for c in range(C):
                        k = a0 + 2 * h + c
                        fill_a(k)
                        nc.tensor.matmul(A[k % 2][:, 0:kw], q_T[c * QD:(c + 1) * QD, h, t * P:(t + 1) * P],
                                         k_T[c * QD:(c + 1) * QD, h, 0:kw], start=True, stop=True
                                         ).then_inc(a_full[k % 2], 1)
                    yield
                    yield
                    pe.wait_ge(comb_done, H * t + h + 1)
                    transposes(t0 + h, a_tok, P, t + 1)
                    yield
                values(s, H - 1)
                yield
                yield
                pe.wait_ge(on_done, t + 1)
                transposes(t0 + H, a_tok, P, 4)
                yield

            def part_l(s):
                u, n, r = tail_no(s), rows_of(s), row0[s]
                z = mix_T[:, H:2 * H, r:r + n]
                if s:
                    pe.wait_ge(conv_done, s)
                else:
                    pe.wait_ge(sample_conv_done, 2)
                after(pe, zc_done, u)
                for ct in range(CT):
                    m = nc.tensor.matmul(M[:, 0:n], ones[:, :], z[:, ct, :], start=(ct == 0), stop=(ct == CT - 1))
                m.then_inc(mean_done, 1)
                yield
                yield
                pe.wait_ge(zsq_done, u + 1)
                sq = exps[0][:, :].rearrange("p (c n) -> p c n", c=CT)
                for ct in range(CT):
                    m = nc.tensor.matmul(M[:, P:P + n], ones[:, :], sq[:, ct, 0:n], start=(ct == 0),
                                         stop=(ct == CT - 1))
                m.then_inc(var_done, 1)
                yield
                yield

            def part_w(s):
                u, n, r, a0 = tail_no(s), rows_of(s), row0[s], base[("W", s)][0]
                pe.wait_ge(mix_done, u + 1)
                if u == 0:
                    pe.wait_ge(wout_in, 16)
                if s:
                    pe.wait_ge(*filled(t_free, base[("Q", s)][1] + H))
                for c in range(2):
                    k = a0 + c
                    fill_a(k)
                    for kt in range(KT):
                        m = nc.tensor.matmul(A[k % 2][0:n, :], mix_T[:, kt, r:r + n],
                                             w_out_sb[:, kt, c * 512:(c + 1) * 512],
                                             start=(kt == 0), stop=(kt == KT - 1))
                        if kt == KT - 1:
                            m.then_inc(a_full[k % 2], 1)
                        if kt % 4 == 3:
                            yield

            def part_r(s):
                u, n, (a0, t0, hn) = tail_no(s), rows_of(s), base[("R", s)]
                yield
                transpose_h(("R", s), n)
                yield
                for q in range(2):
                    pe.wait_ge(t_free[(t0 + q) % 2], (t0 + q) // 2 + 1)
                after(pe, logit_read, u)
                if u == 0:
                    pe.wait_ge(rw_in, 16)
                for kt in range(KT):
                    m = nc.tensor.matmul(M[0:n, 256:256 + E], h_T[:, kt, 0:n], r_w[:, kt, :],
                                         start=(kt == 0), stop=(kt == KT - 1))
                m.then_inc(logits_done, 1)
                yield
                yield
                pe.wait_ge(gate_done, u + 1)
                for v in range(u):
                    nc.tensor.matmul(M[0:n, 288:288 + E], ones[:, 0:n], chosen[:, v, :], start=(v == 0),
                                     stop=False)
                nc.tensor.matmul(M[0:n, 288:288 + E], upper[0:n, 0:n], chosen[0:n, u, :], start=(u == 0),
                                 stop=True).then_inc(rank_done, 1)
                pe.transpose(M[0:E, 320:320 + n], gsum[0:n, :], ident[0:n, 0:n]).then_inc(gT_done, 1)
                yield
                pe.wait_ge(gT_copied, u + 1)
                if u == 0:
                    pe.wait_ge(bd_in, 16)
                for c in range(2):
                    k = a0 + c
                    fill_a(k)
                    nc.tensor.matmul(A[k % 2][0:n, :], g_T[:, 0:n], bd[:, c * 512:(c + 1) * 512],
                                     start=True, stop=True).then_inc(a_full[k % 2], 1)
                yield

            def sample_out(b):
                pe.wait_ge(us_done, b + 1)
                nc.tensor.matmul(S7[:, 256 + 4 * b:260 + 4 * b], us[:, :], coef[:, :], start=True, stop=True
                                 ).then_inc(ot_done, 1)

            def sample_step(b, g):
                if b < 0:
                    return
                if g == 0:
                    pe.wait_ge(pm_done, b + 1)
                    pe.transpose(S7[0:HC, 0:P], pmax[:, :], ident[:, :]).then_inc(small_pe, 1)
                if g == 1:
                    pe.wait_ge(gm_ready, b + 1)
                    nc.tensor.matmul(S7[:, P:P + HC], ones[0:HC, :], dg[:, :], start=True, stop=True
                                     ).then_inc(small_pe, 1)
                if g == 2 and b:
                    sample_out(b - 1)
                if g == 4:
                    pe.wait_ge(es_done, b + 1)
                    nc.tensor.matmul(S7[:, P + HC:P + HC + 1], e_pad[:, :, :].rearrange("p h n -> p (h n)"),
                                     ones[:, 0:1], start=True, stop=True).then_inc(small_pe, 1)
                for gg in V_OF_STEP.get(g, ()):
                    if gg == 0:
                        pe.wait_ge(exp_done, b + 1)
                        after(pe, us_done, b)
                    use = 4 * b + gg // RING + 1
                    pe.wait_ge(v_full[gg % RING], 16 * GP * use)
                    for p in range(GP):
                        page = gg * GP + p
                        for h in range(H):
                            m = nc.tensor.matmul(U[32 * h:32 * h + C, 0:VD], ex[:, page, C * h:C * h + C],
                                                 v_ring[:, gg % RING, p, h * VD:(h + 1) * VD],
                                                 start=(page == 0), stop=False)
                    m.then_inc(pv_done, 1)
                if g == NG - 1:
                    pe.wait_ge(vn_in, 16 * (b + 1))
                    for h in range(H):
                        m = nc.tensor.matmul(U[32 * h:32 * h + C, 0:VD], ex[0:1, PAGES, C * h:C * h + C],
                                             v_new[0:1, h * VD:(h + 1) * VD], start=False, stop=True)
                    m.then_inc(u_all, 1)

            pe.wait_ge(pool_consts, 1)
            pe.wait_ge(cmap_done, 1)
            for _ in part_p(0):
                pass
            part_c()
            parts = {"P": part_p, "Q": part_q, "L": part_l, "W": part_w, "R": part_r}
            run_with_samples(sample_step, (x for kind, s in ORDER[2:-4] for x in parts[kind](s)))
            sample_out(NB - 1)
            pe.wait_ge(otss_done, 1)
            nc.tensor.matmul(M[:, 448:480], ones[:, :], ot_sq[:, :], start=True, stop=True).then_inc(otsq_done, 1)
            for kind, s in ORDER[-3:]:
                for _ in parts[kind](s):
                    pass
            for v in range(TILES + 1):
                n = P if v < TILES else NB
                m = nc.tensor.matmul(M[:, 288:288 + E], ones[0:n, :], chosen[0:n, v, :], start=(v == 0),
                                     stop=(v == TILES))
            m.then_inc(counts_done, 1)

            G = [[PS[0], PS[1]], [PS[2], PS[3]]]
            Y = [PS[4], PS[5]]
            XB = [PS[6], PS[2]]
            AB = [PS[6], PS[7]]

            def transpose_x(i):
                pe.wait_ge(gathered, i * 16 + 16)
                for q in range(2):
                    for k in range(4):
                        m = pe.transpose(XB[q][:, k * P:(k + 1) * P], xg[:, (4 * q + k) * P:(4 * q + k + 1) * P],
                                         ident[:, :])
                    m.then_inc(xt_full, 1)

            def gate_up(i, half):
                g, u = G[half]
                after(pe, gclip_done, i * 2 + (half - 1))
                if half == 0:
                    pe.wait_ge(sel_done, i + 1)
                    pe.wait_ge(xt_copied, i * 2 + 2)
                for part, bank in enumerate((g, u)):
                    nc.tensor.matmul(bank[:, :], sel[0:96, :], b_split[0:96, part * F + half * 512:
                                                                      part * F + half * 512 + 512],
                                     start=True, stop=False)
                for kq in range(2):
                    c = 2 * half + kq
                    pe.wait_ge(w_full[c], i * 32 + 32)
                    for k in range(4):
                        for part, bank in enumerate((g, u)):
                            m = nc.tensor.matmul(bank[:, :], hg_T[:, 4 * kq + k, :], gu_chunk[c][:, k, part, :],
                                                 start=False, stop=(kq == 1 and k == 3))
                    m.then_inc(w_used[c], 1)

            def down(i, half):
                c = 4 + half
                pe.wait_ge(at_copied, i * 2 + (half + 1))
                pe.wait_ge(w_full[c], i * 16 + 16)
                if half == 0:
                    after(pe, y_copied, i)
                for k in range(4):
                    for n in range(2):
                        m = nc.tensor.matmul(Y[n][:, :], act_T[:, 4 * half + k, :],
                                             dn_chunk[half][:, k, n * 512:(n + 1) * 512],
                                             start=(half == 0 and k == 0), stop=(half == 1 and k == 3))
                m.then_inc(w_used[c], 1)

            def transpose_act(i, half):
                pe.wait_ge(act_done, i * 2 + (half + 1))
                for k in range(4):
                    m = pe.transpose(AB[half][:, k * P:(k + 1) * P], act_tok[:, k * P:(k + 1) * P], ident[:, :])
                m.then_inc(at_full, 1)

            def expert_block(i):
                gate_up(i, 0)
                gate_up(i, 1)
                transpose_act(i, 0)
                down(i, 0)
                transpose_act(i, 1)
                transpose_x(i + 1)
                down(i, 1)

            transpose_x(0)
            expert_block(0)
            with pe.Fori(1, E) as i:
                expert_block(i)
            pe.wait_ge(meta_out, 1)
            n = pe.value_load(n_ovf[0:1, 0:1], min_val=0, max_val=OVF)
            with pe.Fori(0, OVF) as j:
                with pe.If(j < n):
                    expert_block(j + E)

        @block.vector
        def _(dve):
            V = Chain(dve, dve_step)

            def add(out, a, b, op=ALU.add):
                return nc.vector.tensor_tensor(out, a, b, op)

            def mul(out, a, b):
                return nc.vector.tensor_tensor(out, a, b, ALU.mult)

            def total(out, src):
                return nc.vector.tensor_reduce(out, src, X, ALU.add)

            dve.wait_ge(lam_in, 64)
            pairs = lam4[:, :, :].rearrange("p (a b) n -> p a b n", a=2)
            V.link(mul(pairs[:, :, 0, :], pairs[:, :, 0, :], pairs[:, :, 1, :]))
            total(stl[:, 2:4], pairs[:, :, 0, :]).then_inc(ss16_done, 1)
            dve.wait_ge(pool_consts, 1)
            V.link(nc.vector.memset(U[:, :], 0.0))
            V.link(total(pad1[:, :], cmap[:, :, :].rearrange("p c h -> p (c h)")))
            V.link(nc.vector.tensor_scalar(pad1[:, :], pad1[:, :], -1.0, 1.0, ALU.mult, ALU.add))
            dve.wait_ge(r16_done, 1)
            V.link(add(nlam[:, :], stl[:, 5:6], stl[:, 4:5], ALU.subtract))
            V.link(nc.vector.tensor_scalar(nlam[:, :], nlam[:, :], -LAM_INIT, None, ALU.add))
            nc.vector.scalar_tensor_tensor(cmap[:, 0, :], cmap[:, 1, :], nlam[:, :], cmap[:, 0, :],
                                           ALU.mult, ALU.add).then_inc(cmap_done, 1)
            dve.wait_ge(norm1_in, 16)

            def scale_rows(part, src, n):
                hn = base[part][2]
                dve.wait_ge(rstd_done, hn + 1)
                nc.vector.scalar_tensor_tensor(h_tok[0:n, :], src[0:n, :], stn[0:n, 2:3], norm_b[0:n, :],
                                               ALU.mult, ALU.mult).then_inc(h_done, 1)

            def part_p(s):
                n, (a0, t0, _h) = rows_of(s), base[("P", s)]
                qk3 = qk[0:n, :].rearrange("p (g d) -> p g d", d=QD)
                rot3 = rot[0:n, :].rearrange("p (g d) -> p g d", d=QD)
                qk4 = qk[0:n, :].rearrange("p (a g d) -> p a g d", a=2, d=QD)
                rot4 = rot[0:n, :].rearrange("p (a g d) -> p a g d", a=2, d=QD)
                scale_rows(("P", s), x_in, n)
                yield
                yield
                yield from [None] * 3
                for c in range(2):
                    dve.wait_ge(*filled(a_free, a0 + c))
                if s == 1:
                    dve.wait_ge(sample_rows_out, 64)
                if s > 1:
                    dve.wait_ge(*filled(t_full, base[("Q", s - 1)][1] + H))
                    dve.wait_ge(o_full, H * (s - 1))
                V.link(mul(rot[0:n, :], qk[0:n, :], qk[0:n, :]))
                total(stp[0:n, 0:16], rot3).then_inc(ss16_done, 1)
                yield
                if s == 0:
                    dve.wait_ge(setup_in, 16 * 11)
                for i in range(2):
                    V.link(mul(cw[0:n, i, :].rearrange("p (a n) -> p a n", n=32),
                               rope[0:n, s, i:i + 1, :].to_broadcast([n, 4, 32]),
                               wqk[0:n, :, :].rearrange("p a (b n) -> p (a b) n", n=32)))
                yield
                dve.wait_ge(r16_done, s + 2)
                V.link(mul(qk3, qk3, stp[0:n, 32:48].unsqueeze(2).to_broadcast([n, 16, QD])))
                yield
                cos, sin = [cw[0:n, i, :].rearrange("p (a d) -> p a d", a=2).unsqueeze(2).to_broadcast(
                    [n, 2, HC, QD]) for i in range(2)]
                V.link(mul(rot4, qk4, cos))
                V.link(mul(qk4, qk4, sin))
                yield
                V.link(add(rot3[:, :, 0:32], rot3[:, :, 0:32], qk3[:, :, 32:64], ALU.subtract))
                add(rot3[:, :, 32:64], rot3[:, :, 32:64], qk3[:, :, 0:32]).then_inc(rot_done, 1)
                dve.wait_ge(rot_done, s + 1)
                if s == 0:
                    V.link(mul(qk[0:n, 0:AW], rot[0:n, 0:AW], rot[0:n, AW:]))
                    total(snw[0:n, :], qk3[:, 0:HC, :]).then_inc(kmul_done, 1)
                    dve.wait_ge(kmul_done, 1)
                yield
                yield
                dve.wait_ge(*filled(a_free, a0 + 4))
                V.link(nc.vector.tensor_scalar(u_tok[0:n, :], u_tok[0:n, :], 1.0, None, ALU.add))
                V.link(nc.vector.reciprocal(u_tok[0:n, :], u_tok[0:n, :]))
                dve.wait_ge(*filled(a_full, a0 + 3))
                k = a0 + 3
                mul(u_tok[0:n, :], A[k % 2][0:n, :], u_tok[0:n, :]).then_inc(a_free[k % 2], 1)
                yield
                yield
                yield

            def part_c():
                t0 = base[("C", 0)][1]
                dve.wait_ge(*filled(t_free, t0))
                V.link(nc.vector.tensor_scalar(sub_w[:, :], vec_T[:, 12:13], 1.0 - LAM_INIT, None, ALU.mult))
                V.link(nc.vector.tensor_scalar(neg_gb[:, :], vec_T[:, 4:12], -1.0, None, ALU.mult))
                for k in (base[("P", 0)][1] + 2, t0 + 1, t0 + 2, t0 + 3):
                    dve.wait_ge(*filled(t_free, k))
                V.link(mul(sext, sext, w_T[:, :, :].unsqueeze(2).to_broadcast([P, CT, NB, TAPS])))
                V.link(total(zs[:, :, :], sext))
                add(zs[:, :, :], zs[:, :, :], vec_T[:, 0:4].unsqueeze(2).to_broadcast([P, CT, NB])
                    ).then_inc(sample_conv_done, 1)
                dve.wait_ge(sample_conv_done, 1)

            def part_q(s):
                t, (a0, t0, _h) = s - 1, base[("Q", s)]
                kw = (t + 1) * P
                for h in range(H):
                    for c in range(C):
                        k = a0 + 2 * h + c
                        dve.wait_ge(*filled(a_full, k))
                        diag = A[k % 2][:, t * P:(t + 1) * P]
                        V.link(add(diag, diag, cmask[:, :]))
                        V.link(nc.vector.reduce_max(stq[:, c:c + 1], A[k % 2][:, 0:kw], X))
                    nc.vector.tensor_scalar(stq[:, 2:4], stq[:, 0:2], -SM_SCALE, None, ALU.mult
                                            ).then_inc(max_done, 1)
                    yield
                    for c in range(C):
                        dve.wait_ge(*filled(a_free, a0 + 2 * h + c))
                    V.link(nc.vector.reciprocal(stq[:, 6:8], stq[:, 4:6]))
                    V.link(mul(stq[:, 7:8], stq[:, 7:8], nlam[:, :]))
                    if h:
                        dve.wait_ge(*filled(t_full, t0 + h - 1))
                    else:
                        dve.wait_ge(k_out, 16 * s)
                        for k in (2, 3):
                            dve.wait_ge(*filled(t_full, base[("P", s)][1] + k))
                    V.link(nc.vector.tensor_scalar(a_tok[:, 0:kw], exps[0][:, 0:kw], stq[:, 6:7], None, ALU.mult))
                    nc.vector.scalar_tensor_tensor(a_tok[:, 0:kw], exps[1][:, 0:kw], stq[:, 7:8], a_tok[:, 0:kw],
                                                   ALU.mult, ALU.add).then_inc(comb_done, 1)
                    yield
                    yield
                dve.wait_ge(osq_done, t + 1)
                total(stq[:, 8:12], a_tok.rearrange("p (h n) -> p h n", h=H)).then_inc(oss_done, 1)
                yield
                dve.wait_ge(or_done, t + 1)
                mul(a_tok.rearrange("p (h n) -> p h n", h=H), O[:, :].rearrange("p (h n) -> p h n", h=H),
                    stq[:, 16:20].unsqueeze(2).to_broadcast([P, H, VD])).then_inc(on_done, 1)
                yield
                yield

            def part_l(s):
                u, n, r = tail_no(s), rows_of(s), row0[s]
                z = mix_T[:, H:2 * H, r:r + n]
                e3 = exps[0][:, :].rearrange("p (c n) -> p c n", c=CT)[:, :, 0:n]
                dve.wait_ge(mean_done, u + 1)
                nc.vector.scalar_tensor_tensor(z, M[:, 0:n].unsqueeze(1).to_broadcast([P, CT, n]), -1.0 / CH, z,
                                               ALU.mult, ALU.add).then_inc(zc_done, 1)
                yield
                yield
                dve.wait_ge(vr_done, u + 1)
                mul(z, z, exps[1][:, P:P + n].unsqueeze(1).to_broadcast([P, CT, n])).then_inc(zn_done, 1)
                yield
                dve.wait_ge(ez_done, u + 1)
                for ct in range(CT):
                    V.link(nc.vector.tensor_scalar(z[:, ct, :], z[:, ct, :], vec_T[:, 4 + ct:5 + ct],
                                                   vec_T[:, 8 + ct:9 + ct], ALU.mult, ALU.add))
                V.link(nc.vector.tensor_scalar(e3, e3, 1.0, None, ALU.add))
                V.link(nc.vector.reciprocal(e3, e3))
                mul(z, z, e3).then_inc(mix_done, 1)
                yield

            def part_w(s):
                u, n, a0 = tail_no(s), rows_of(s), base[("W", s)][0]
                for c in range(2):
                    yield
                    k = a0 + c
                    dve.wait_ge(*filled(a_full, k))
                    if c == 0:
                        dve.wait_ge(xw_loaded, 16 * (u + 1))
                    cols = slice(c * 512, (c + 1) * 512)
                    add(x2[0:n, cols], x2[0:n, cols], A[k % 2][0:n, :]).then_inc(a_free[k % 2], 1)
                    yield

            def part_r(s):
                u, n, (a0, t0, hn) = tail_no(s), rows_of(s), base[("R", s)]
                if u == 0:
                    dve.wait_ge(norm2_in, 16)
                    V.link(nc.vector.memset(onehot[:, :, :, :], 0.0))
                    V.link(nc.vector.memset(rankk[:, :, :], 0.0))
                scale_rows(("R", s), x2, n)
                yield
                yield
                dve.wait_ge(logits_done, u + 1)
                add(logit[0:n, :], M[0:n, 256:256 + E], r_b[0:n, :]).then_inc(logit_read, 1)
                dve.wait_ge(logit_read, u + 1)
                V.link(nc.vector.max(top8[0:n, :], logit[0:n, :]))
                V.link(nc.vector.max_index(idx8[0:n, :], top8[0:n, :], logit[0:n, :]))
                V.link(nc.vector.tensor_copy(idxf[0:n, :], idx8[0:n, :]))
                nc.vector.tensor_scalar(str_[0:n, 0:1], top8[0:n, 0:1], -1.0, None, ALU.mult).then_inc(gexp_ask, 1)
                yield
                dve.wait_ge(gexp_done, u + 1)
                V.link(nc.vector.reciprocal(str_[0:n, 2:3], str_[0:n, 1:2]))
                V.link(nc.vector.tensor_scalar(gates[0:n, u, :], str_[0:n, 4:8], str_[0:n, 2:3], None, ALU.mult))
                for k in range(TOPK):
                    V.link(nc.vector.tensor_scalar(onehot[0:n, u, k, :], iota_e[0:n, :], idxf[0:n, k:k + 1], None,
                                                   ALU.is_equal))
                V.link(total(chosen[0:n, u, :], onehot[0:n, u, :, :].rearrange("p k e -> p e k")))
                V.link(mul(gtmp[0:n, :, :], onehot[0:n, u, :, :],
                           gates[0:n, u, :].unsqueeze(2).to_broadcast([n, TOPK, E])))
                total(gsum[0:n, :], gtmp[0:n, :, :].rearrange("p k e -> p e k")).then_inc(gate_done, 1)
                yield
                dve.wait_ge(rank_done, u + 1)
                dve.wait_ge(gate_done, u + 1)
                dve.wait_ge(gT_done, u + 1)
                V.link(mul(gtmp[0:n, :, :], onehot[0:n, u, :, :],
                           M[0:n, 288:288 + E].unsqueeze(1).to_broadcast([n, TOPK, E])))
                V.link(total(rankk[0:n, u, :], gtmp[0:n, :, :]))
                nc.vector.tensor_copy(g_T[:, 0:n], M[0:E, 320:320 + n]).then_inc(gT_copied, 1)
                yield
                for c in range(2):
                    k = a0 + c
                    dve.wait_ge(*filled(a_full, k))
                    cols = slice(c * 512, (c + 1) * 512)
                    add(x2[0:n, cols], x2[0:n, cols], A[k % 2][0:n, :]).then_inc(a_free[k % 2], 1)
                yield

            def sample_step(b, g):
                kb = b + 1
                if kb < NB:
                    r = g % RING
                    if g == 0:
                        dve.wait_ge(qb_in, 32 if kb == 0 else 16 * (kb + 1))
                        if kb == 0:
                            dve.wait_ge(sn_in, 16)
                        V.link(nc.vector.tensor_copy(sc[0:1, kb % 2, PAGES, :], s_new[0:1, kb * HC:(kb + 1) * HC]))
                    dve.wait_ge(k_full[r], 16 * GP * (4 * kb + g // RING + 1))
                    V.link(mul(k_ring[:, r, :, :], k_ring[:, r, :, :],
                               q_b[:, kb % 2, :].unsqueeze(1).to_broadcast([P, GP, AW])))
                    total(sc[:, kb % 2, GP * g:GP * (g + 1), :],
                          k_ring[:, r, :, :].rearrange("p g (h d) -> p g h d", d=QD)).then_inc(kred_done, 1)
                    if g == NG - 1:
                        dve.wait_ge(kred_done, NG * (kb + 1))
                        if kb:
                            dve.wait_ge(small_pe, 3 * (kb - 1) + 1)
                        nc.vector.tensor_reduce(pmax[:, :], sc[:, kb % 2, :, :].rearrange("p g e -> p e g"), X,
                                                ALU.max).then_inc(pm_done, 1)
                if b >= 0 and g == 0:
                    dve.wait_ge(small_pe, 3 * b + 1)
                    V.link(nc.vector.reduce_max(mx[:, :], S7[0:HC, 0:P], X))
                    nc.vector.tensor_scalar(dg[:, :], ident[0:HC, 0:HC], mx[:, :], None, ALU.mult
                                            ).then_inc(gm_ready, 1)
                if b >= 0 and g == 1:
                    dve.wait_ge(small_pe, 3 * b + 2)
                    add(sc[:, b % 2, :, :], sc[:, b % 2, :, :],
                        S7[:, P:P + HC].unsqueeze(1).to_broadcast([P, PAGES + 1, HC]), ALU.subtract
                        ).then_inc(sub_done, 1)
                    if b:
                        copy_u(b - 1)
                if b >= 0 and g == 2:
                    dve.wait_ge(exp_done, b + 1)
                    if b:
                        dve.wait_ge(small_pe, 3 * b)
                    total(e_pad[:, :, 0:C], ex[:, :, :].rearrange("p g (h c) -> p h c g", c=C)
                          ).then_inc(es_done, 1)
                if b >= 0 and g == 5:
                    dve.wait_ge(small_pe, 3 * b + 3)
                    V.link(add(rl[:, :], S7[:, P + HC:P + HC + 1], pad1[:, :]))
                    V.link(nc.vector.reciprocal(rl[:, :], rl[:, :]))
                    if b:
                        dve.wait_ge(ot_done, b)
                    V.link(nc.vector.tensor_scalar(coef[:, :], cmap[:, 0, :], rl[:, :], None, ALU.mult))

            def copy_u(b):
                dve.wait_ge(u_all, b + 1)
                nc.vector.tensor_copy(us[:, :], U[:, 0:VD]).then_inc(us_done, 1)

            for _ in part_p(0):
                pass
            part_c()
            parts = {"P": part_p, "Q": part_q, "L": part_l, "W": part_w, "R": part_r}
            run_with_samples(sample_step, (x for kind, s in ORDER[2:-4] for x in parts[kind](s)))
            copy_u(NB - 1)
            dve.wait_ge(ot_done, NB)
            V.link(nc.vector.tensor_copy(ot[:, :], S7[:, 256:256 + H * NB]))
            mul(ot_sq[:, :], ot[:, :], ot[:, :]).then_inc(otss_done, 1)
            V.link(nc.vector.tensor_copy(mix_T[:, H:2 * H, SEQ:TOK], zs[:, :, :]))
            dve.wait_ge(otr_done, 1)
            V.link(mul(ot[:, :], ot[:, :], sto[:, 0:H * NB]))
            nc.vector.tensor_scalar(mix_T[:, 0:H, SEQ:TOK], ot[:, :].rearrange("p (b h) -> p h b", h=H),
                                    sub_w[:, :], None, ALU.mult).then_inc(sample_conv_done, 1)
            for kind, s in ORDER[-3:]:
                for _ in parts[kind](s):
                    pass

            dve.wait_ge(counts_done, 1)
            c0, c1, c2 = cnt[:, 0, :], cnt[:, 1, :], cnt[:, 2, :]
            V.link(nc.vector.tensor_copy(c0, M[:, 288:288 + E]))
            V.link(nc.vector.tensor_scalar(c1, c0, float(CAP), None, ALU.is_gt))
            for m in range(2, -(-TOK // CAP)):
                V.link(nc.vector.scalar_tensor_tensor(c1, c0, float(m * CAP), c1, ALU.is_gt, ALU.add))
            V.link(nc.vector.tensor_tensor_scan(c2, ones[:, 0:E], c1, 0.0, ALU.mult, ALU.add))
            V.link(add(c1, c2, c1, ALU.subtract))
            TT5 = TILES + 1
            all_k = [P, TT5 * TOPK, E]
            oh = onehot[:, :, :, :].rearrange("p t k e -> p (t k) e")
            rk = rankk[:, :, :].rearrange("p t k -> p (t k)")
            V.link(mul(big, oh, c1.unsqueeze(1).to_broadcast(all_k)))
            V.link(total(ad[:, 0, :], big))
            V.link(mul(big, oh, iota_e[:, :].unsqueeze(1).to_broadcast(all_k)))
            V.link(total(ad[:, 1, :], big))
            V.link(nc.vector.tensor_scalar(ad[:, 2, :], rk, float(CAP), None, ALU.is_ge))
            V.link(nc.vector.tensor_copy(ad[:, 3, :], ad[:, 2, :]))
            for m in range(2, -(-TOK // CAP)):
                V.link(nc.vector.scalar_tensor_tensor(ad[:, 2, :], rk, float(m * CAP), ad[:, 2, :],
                                                      ALU.is_ge, ALU.add))
            V.link(add(ad[:, 0, :], ad[:, 0, :], ad[:, 2, :]))
            V.link(add(ad[:, 0, :], ad[:, 0, :], ad[:, 1, :], ALU.subtract))
            V.link(nc.vector.scalar_tensor_tensor(ad[:, 0, :], ad[:, 0, :], float(E - 1), ad[:, 3, :],
                                                  ALU.add, ALU.mult))
            V.link(add(ad[:, 0, :], ad[:, 0, :], ad[:, 1, :]))
            V.link(nc.vector.scalar_tensor_tensor(ad[:, 2, :], ad[:, 2, :], float(-CAP), rk, ALU.mult, ALU.add))
            V.link(nc.vector.scalar_tensor_tensor(ad[:, 0, :], ad[:, 2, :], float(TCOLS), ad[:, 0, :],
                                                  ALU.mult, ALU.add))
            dve.wait_ge(v_out, 16 * TILES)
            dve.wait_ge(table_zeroed, 16)
            nc.vector.tensor_copy(addr, ad[:, 0, :]).then_inc(addr_done, 1)
            ec = big[0:1, 0:OVF + 1, :]
            V.link(nc.vector.tensor_tensor(ec, c2[0:1, :].unsqueeze(1).to_broadcast([1, OVF + 1, E]),
                                           iota_o[0:1, :].unsqueeze(2).to_broadcast([1, OVF + 1, E]), ALU.is_le))
            V.link(total(ef[0:1, E:TCOLS], ec))
            V.link(nc.vector.tensor_scalar(ef[0:1, E:TCOLS], ef[0:1, E:TCOLS], float(E - 1), None, ALU.min))
            V.link(nc.vector.tensor_copy(ef[0:1, 0:E], iota_e[0:1, :]))
            V.link(nc.vector.tensor_copy(e_tab, ef[0:1, :]))
            nc.vector.tensor_copy(n_ovf, c2[0:1, E - 1:E]).then_inc(meta_out, 1)
            dve.wait_ge(meta_out, 1)

            dve.wait_ge(bias_in, 48)
            V.link(nc.vector.tensor_copy(b_split[0:96, :], b_stage[0:96, :]))
            V.link(add(b_stage[0:96, :], b_stage[0:96, :], b_split[0:96, :], ALU.subtract))
            V.link(nc.vector.tensor_copy(b_split[32:64, :], b_stage[32:64, :]))
            V.link(nc.vector.tensor_copy(b_split[64:96, :], b_stage[64:96, :]))
            V.link(add(b_stage[64:96, :], b_stage[64:96, :], b_split[64:96, :], ALU.subtract))
            V.link(nc.vector.tensor_copy(b_split[64:96, :], b_stage[64:96, :]))
            for q in range(3):
                V.link(nc.vector.tensor_copy(pick3[32 * q:32 * q + 32, :], ident[32 * q:32 * q + 32,
                                                                              32 * q:32 * q + 32]))

            def select(i):
                e = dve.value_load(e_tab[0:1, bass.ds(i, 1)], min_val=0, max_val=E - 1)
                nc.vector.tensor_copy(sel[0:96, :], pick3[0:96, bass.ds(e, 1)].to_broadcast([96, P])
                                      ).then_inc(sel_done, 1)

            select(0)
            dve.wait_ge(table_in, 16)
            nc.vector.tensor_scalar(slot_tok, slots, 2, None, ALU.logical_shift_right).then_inc(idx_done, 1)

            def expert_block(i):
                for half in range(2):
                    dve.wait_ge(w_used[2 * half + 1], i + 1)
                    g, u = (PS[0], PS[1]) if half == 0 else (PS[2], PS[3])
                    V.link(nc.vector.tensor_scalar(g_act, g[:, :], LIMIT, None, ALU.min))
                    nc.vector.tensor_scalar(u_act, u[:, :], LIMIT, -LIMIT, ALU.min, ALU.max
                                            ).then_inc(gclip_done, 1)
                    dve.wait_ge(gclip_done, i * 2 + (half + 1))
                    V.link(nc.vector.scalar_tensor_tensor(u_act, u_act, 1.0, g_act, ALU.add, ALU.mult))
                    dve.wait_ge(sig_done, i * 2 + (half + 1))
                    after(dve, at_full, i * 2 + half)
                    mul(act_tok, u_act, s_act).then_inc(act_done, 1)
                    dve.wait_ge(act_done, i * 2 + (half + 1))
                select(i + 1)
                dve.wait_ge(w_used[5], i + 1)
                after(dve, y_scattered, i * 16)
                V.link(nc.vector.tensor_copy(y_sb[:, 0:512], PS[4][:, :]))
                nc.vector.tensor_copy(y_sb[:, 512:], PS[5][:, :]).then_inc(y_copied, 1)

            start = V.base + V.n
            V.base, V.n = start, 0
            expert_block(0)
            steps = V.n
            with dve.Fori(1, E) as i:
                V.base, V.n = i * steps + start, 0
                expert_block(i)
            n = dve.value_load(n_ovf[0:1, 0:1], min_val=0, max_val=OVF)
            with dve.Fori(0, OVF) as j:
                with dve.If(j < n):
                    V.base, V.n = j * steps + (start + E * steps), 0
                    expert_block(j + E)

            for u, s in enumerate(TAIL):
                m, b = rows_of(s), u % 2
                dve.wait_ge(y_loaded[b], 32 * (u // 2 + 1))
                acc = out_rows[b][0:m, TOPK * D:]
                for k in range(TOPK):
                    nc.vector.scalar_tensor_tensor(acc, out_rows[b][0:m, k * D:(k + 1) * D], gates[0:m, u, k:k + 1],
                                                   acc, ALU.mult, ALU.add).then_inc(pair_done, 1)
                    dve.wait_ge(pair_done, u * TOPK + k + 1)


_INS = ["x_prompt", "x_sample", "cache_k", "cache_v", "state_conv", "page_table", "norm1_w", "w_in", "q_norm_w",
        "k_norm_w", "lambda_q1", "lambda_k1", "lambda_q2", "lambda_k2", "subln_w", "conv_w", "conv_b", "conv_ln_g",
        "conv_ln_b", "w_out", "norm2_w", "router_w", "router_b", "w_gate_up", "b_gate_up", "w_down", "b_down"]
_OUTS = [(1, 512, 1024), (8, 1, 1024), (1, 1, 512, 4, 2, 64), (1, 1, 512, 4, 128), (1, 1, 30, 512),
         (1, 8, 1, 4, 2, 64), (1, 8, 1, 4, 128), (1, 8, 30, 512)]


def _rope_table():
    half = QD // 2
    inv = np.power(np.float32(10000.0), -np.arange(half, dtype=np.float32) / np.float32(half)).astype(np.float32)
    pos = np.concatenate([np.arange(SEQ), np.full(NB, PAGES * PAGE)]).astype(np.float32)
    ang = (pos[:, None] * inv[None, :]).astype(np.float32)
    return np.stack([np.cos(ang), np.sin(ang)], axis=1).astype(np.float32)


def kernel(**inputs):
    import numpy as _np
    import concourse.bacc as _bacc
    from concourse import mybir as _mybir
    from concourse.bass_utils import run_bass_kernel_spmd as _run

    nc = _bacc.Bacc("TRN2", target_bir_lowering=False, num_devices=1)
    arrays, args = {}, []
    for name in _INS:
        a = _np.ascontiguousarray(inputs[name])
        arrays[f"in_{name}"] = a
        args.append(nc.dram_tensor(f"in_{name}", a.shape, _mybir.dt.from_np(a.dtype), kind="ExternalInput").ap())
    table = _rope_table()
    arrays["rope_table"] = table
    fp32, i32 = _mybir.dt.float32, _mybir.dt.int32
    args.append(nc.dram_tensor("rope_table", table.shape, fp32, kind="ExternalInput").ap())
    for i, shape in enumerate(_OUTS):
        args.append(nc.dram_tensor(f"out_{i}", shape, fp32, kind="ExternalOutput").ap())
    for name, shape, dt in (("h2_rows", (TOK, D), fp32), ("x2_rows", (TOK, D), fp32), ("y_rows", (PAIRS, D), fp32),
                            ("q_rows", (NB, AW), fp32), ("s_new_rows", (NB, HC), fp32),
                            ("slot_table", (P * TCOLS, 1), i32)):
        args.append(nc.dram_tensor(name, shape, dt, kind="Internal").ap())
    hybrid_step(nc, *args)
    r = _run(nc, [arrays], core_ids=[0])
    return tuple(r.results[0][f"out_{i}"] for i in range(len(_OUTS)))
```

```python
import math
import numpy as np
import concourse.bass as bass
from concourse import mybir
from contextlib import ExitStack

P = 128
D = 1024
KT = D // P
SEQ, NB = 512, 8
TOK = SEQ + NB
TILES = SEQ // P
H, C, QD, VD = 4, 2, 64, 128
HC = H * C
AW = H * VD
CH = 512
CT = CH // P
TAPS = 31
PAGES, PAGE = 32, 128
GP = 2
NG = PAGES // GP
RING = 4
IN_COLS = 2560
E, TOPK, F = 32, 4, 1024
PAIRS = TOK * TOPK
CAP = P
OVF = PAIRS // CAP
BLOCKS = E + OVF
TCOLS = BLOCKS + 1
UNUSED = 1 << 20
LIMIT, ALPHA = 7.0, 1.702
EPS = 1e-6
NEG = -1e30
SM_SCALE = QD ** -0.5
LAM_INIT = 0.8 - 0.6 * math.exp(0.0)


class Chain:

    def __init__(self, eng, sem, base=0):
        self.eng, self.sem, self.base, self.n = eng, sem, base, 0

    def link(self, ins):
        self.n += 1
        ins.then_inc(self.sem, 1)
        self.eng.wait_ge(self.sem, self.base + self.n)


def hybrid_step(nc, x_prompt, x_sample, cache_k, cache_v, state_conv, page_table, norm1_w, w_in,
                q_norm_w, k_norm_w, lambda_q1, lambda_k1, lambda_q2, lambda_k2, subln_w, conv_w,
                conv_b, conv_ln_g, conv_ln_b, w_out, norm2_w, router_w, router_b, w_gate_up,
                b_gate_up, w_down, b_down, rope_table,
                y_prompt, y_sample, new_k_p, new_v_p, new_conv_p, new_k_s, new_v_s, new_conv_s,
                h2_rows, x2_rows, y_rows, q_rows, s_new_rows, slot_table):
    fp32, bf16, i32, u32 = mybir.dt.float32, mybir.dt.bfloat16, mybir.dt.int32, mybir.dt.uint32
    ACT = mybir.ActivationFunctionType
    ALU = mybir.AluOpType
    X = mybir.AxisListType.X
    ctx = ExitStack()
    with ctx:
        def sb(name, shape, dt=fp32):
            return ctx.enter_context(nc.sbuf_tensor(name, shape, dt))

        def sem(name):
            return ctx.enter_context(nc.semaphore(name))

        SLOT = 4096
        wts = sb("wts", [P, 6 * SLOT])
        w_in_sb = wts[:, 0:KT * IN_COLS].rearrange("p (k n) -> p k n", k=KT)
        w_out_sb = wts[:, 0:KT * D].rearrange("p (k n) -> p k n", k=KT)
        k_ring = wts[:, 5 * SLOT:6 * SLOT].rearrange("p (s g n) -> p s g n", s=RING, g=GP)
        v_ring = sb("v_ring", [P, RING, GP, AW])
        x_in = sb("x_in", [P, D])
        x2 = x_in
        h_tok = sb("h_tok", [P, D])
        h_T = sb("h_T", [P, KT, P])
        qk = sb("qk", [P, 2 * AW])
        rot = sb("rot", [P, 2 * AW])
        exps = [qk[:, 0:SEQ], qk[:, SEQ:2 * SEQ]]
        a_tok = rot[:, 0:SEQ]
        a_T = rot[:, SEQ:2 * SEQ]
        v_tok = sb("v_tok", [P, TILES, AW])
        u_tok = sb("u_tok", [P, CH])
        q_T = sb("q_T", [P, H, SEQ])
        k_T = sb("k_T", [P, H, SEQ])
        u_T = sb("u_T", [P, CT, TAPS - 1 + SEQ])
        mix = sb("mix", [P, 2 * H * TOK])
        mix_T = mix[:, :].rearrange("p (k n) -> p k n", k=2 * H)
        sext = mix[:, H * TOK:H * TOK + CT * NB * TAPS].rearrange("p (c b j) -> p c b j", c=CT, b=NB)
        norm_b = sb("norm_b", [P, D])
        q_b = sb("q_b", [P, 2, AW])
        v_new = sb("v_new", [1, AW])
        s_new = sb("s_new", [1, NB * HC])
        sc = sb("sc", [P, 2, PAGES + 1, HC])
        ex = sb("ex", [P, PAGES + 1, HC])
        e_pad = sb("e_pad", [P, H, 32])
        rope = sb("rope", [P, TILES + 1, 2, 32])
        wqk = sb("wqk", [P, 2, QD])
        cw = sb("cw", [P, 2, 2 * QD])
        conv_tmp = sb("conv_tmp", [P, CT * P])
        conv_tmpv = conv_tmp[:, :].rearrange("p (c n) -> p c n", c=CT)
        w_T = sb("w_T", [P, CT, TAPS])
        zs = sb("zs", [P, CT, NB])
        conv_w_in = k_T[0:TAPS, 0, :]
        lam4 = k_T[:, 1, 0:4 * QD].rearrange("p (i n) -> p i n", i=4)
        vecs = k_T[0:16, 2, 0:P]
        state_in = q_T[0:120, 0:2, :]
        vec_T = sb("vec_T", [P, 16])
        neg_gb = sb("neg_gb", [P, 2 * CT])
        sub_w = sb("sub_w", [P, 1])
        ident = sb("ident", [P, P])
        ones = sb("ones", [P, P])
        upper = sb("upper", [P, P])
        cmask = sb("cmask", [P, P])
        cmap = sb("cmap", [P, C, H])
        pad1 = sb("pad1", [P, 1])
        nlam = sb("nlam", [P, 1])
        eps_c = sb("eps_c", [P, 1])
        stl, stn, stp, stq, str_, sto = [sb(n, [P, w]) for n, w in (
            ("stl", 8), ("stn", 4), ("stp", 48), ("stq", 32), ("str_", 16), ("sto", 64))]
        snw = sb("snw", [P, HC])
        pmax = sb("pmax", [P, HC])
        mx = sb("mx", [HC, 1])
        dg = sb("dg", [HC, HC])
        rl = sb("rl", [P, 1])
        coef = sb("coef", [P, H])
        ot = sb("ot", [P, H * NB])
        ot_sq = sb("ot_sq", [P, H * NB])
        us = sb("us", [P, VD])
        ef = sb("ef", [1, TCOLS])
        iota_o = sb("iota_o", [P, OVF + 1])
        pages_sb = sb("pages_sb", [1, NB * PAGES], i32)
        route = q_T[:, 2:4, :].rearrange("p a n -> p (a n)")
        onehot = route[:, 0:640].rearrange("p (t k e) -> p t k e", t=TILES + 1, k=TOPK)
        chosen = route[:, 640:800].rearrange("p (t e) -> p t e", e=E)
        gtmp = route[:, 800:928].rearrange("p (k e) -> p k e", e=E)
        ad = route[:, 928:1008].rearrange("p (a n) -> p a n", a=4)
        r_w = k_T[:, 0, 0:KT * E].rearrange("p (k e) -> p k e", e=E)
        g_T = k_T[0:E, 0, 256:384]
        gsum = k_T[:, 0, 480:480 + E]
        cnt = k_T[:, 0, 384:480].rearrange("p (a e) -> p a e", e=E)
        r_b = sb("r_b", [P, E])
        iota_e = sb("iota_e", [P, E])
        logit = sb("logit", [P, E])
        top8 = sb("top8", [P, 8])
        idx8 = sb("idx8", [P, 8], u32)
        idxf = sb("idxf", [P, 8])
        gates = sb("gates", [P, TILES + 1, TOPK])
        rankk = sb("rankk", [P, TILES + 1, TOPK])
        PS = [ctx.enter_context(nc.psum_tensor(f"bank{i}", [P, 512], fp32)) for i in range(8)]
        A, T, U, O, M, S7 = PS[0:2], PS[2:4], PS[4], PS[5], PS[6], PS[7]

        bd = q_T[0:E, 0:2, :].rearrange("p a n -> p (a n)")
        g_act, u_act, s_act, act_tok = [[q_T[:, n, :], half_row] for n, half_row in enumerate(
            (qk[:, 0:512], qk[:, 512:1024], rot[:, 0:512], rot[:, 512:1024]))]
        act_T = [k_T[:, n, :].rearrange("p (k n) -> p k n", n=P) for n in range(2)]
        y_sb = k_T[:, 2:4, :].rearrange("p a n -> p (a n)")
        xg = h_tok
        hg_T = h_T
        b_stage = mix[0:96, 0:2 * F]
        b_split = u_T[:, :, :].rearrange("p a n -> p (a n)")[:, 0:F].bitcast(bf16)
        sel = v_tok[:, 0, 0:P // 2].bitcast(bf16)
        pick3 = v_tok[:, 0, 64:64 + E // 2].bitcast(bf16)
        slots = v_tok[:, 1, 0:TCOLS].bitcast(i32)
        slot_tok = v_tok[:, 1, 64:64 + TCOLS].bitcast(i32)
        g_idx = v_tok[:, 1, 128:129].bitcast(i32)
        y_idx = v_tok[:, 1, 129:130].bitcast(i32)
        fill_i = v_tok[:, 1, 130:130 + TCOLS].bitcast(i32)
        e_tab = v_tok[0:1, 1, 192:192 + TCOLS].bitcast(i32)
        n_ovf = v_tok[0:1, 1, 250:251].bitcast(i32)
        n_tok = v_tok[0:1, 1, 256:256 + TCOLS].bitcast(i32)
        addr = v_tok[:, 2, 0:20].bitcast(i32)
        pair_id = v_tok[:, 2, 32:52].bitcast(i32)
        tA = v_tok[:, 3, 0:64]
        tB = v_tok[:, 3, 64:128]
        tC = v_tok[:, 3, 128:192]
        big = y_sb[:, 0:(TILES + 1) * TOPK * E].rearrange("p (t e) -> p t e", e=E)
        out_rows = [wts[:, n * 8192:n * 8192 + 5 * D] for n in range(2)]

        ORDER = [("P", 0), ("C", 0)] + [(kind, s) for s in range(1, TILES + 1) for kind in "PQ"] + \
                [(kind, s) for s in range(1, TILES + 1) for kind in "LWR"] + \
                [("O", 0), ("L", 0), ("W", 0), ("R", 0)]
        USES = {"P": (5, 5, 1), "C": (0, 4, 0), "Q": (8, 5, 0), "L": (0, 0, 0), "W": (2, 0, 0), "R": (2, 2, 1),
                "O": (0, 0, 0)}
        TAIL = [1, 2, 3, 4, 0]
        base, a, t, h = {}, 0, 0, 0
        for part in ORDER:
            base[part] = (a, t, h)
            da, dt_, dh = USES[part[0]]
            if part == ("P", 0):
                dt_ = 3
            a, t, h = a + da, t + dt_, h + dh

        def rows_of(s):
            return NB if s == 0 else P

        def tail_no(s):
            return TAIL.index(s)

        x_rows = [x_sample[:, 0, :]] + [x_prompt[0, n * P:(n + 1) * P, :] for n in range(TILES)]
        row0 = [SEQ] + [n * P for n in range(TILES)]
        v_rows = [conv_tmp[0:NB, :]] + [v_tok[:, n, :] for n in range(TILES)]
        kc = cache_k[0].rearrange("n p h c d -> n p (h c d)")
        vc = cache_v[0].rearrange("n p h d -> n p (h d)")
        new_k_rows = [new_k_s[0, :, 0].rearrange("b h c d -> b (h c d)")] + \
                     [new_k_p[0, 0, n * P:(n + 1) * P].rearrange("b h c d -> b (h c d)") for n in range(TILES)]
        new_v_rows = [new_v_s[0, :, 0].rearrange("b h d -> b (h d)")] + \
                     [new_v_p[0, 0, n * P:(n + 1) * P].rearrange("b h d -> b (h d)") for n in range(TILES)]
        y_out = [y_sample[:, 0, :]] + [y_prompt[0, n * P:(n + 1) * P, :] for n in range(TILES)]

        a_full, a_free = [sem(f"a_full{n}") for n in range(2)], [sem(f"a_free{n}") for n in range(2)]
        t_full, t_free = [sem(f"t_full{n}") for n in range(2)], [sem(f"t_free{n}") for n in range(2)]
        k_full = [sem(f"k_full{n}") for n in range(RING)]
        v_full = [sem(f"v_full{n}") for n in range(RING)]
        w_full = [sem(f"w_full{n}") for n in range(6)]
        w_used = [sem(f"w_used{n}") for n in range(6)]
        y_loaded = [sem(f"y_loaded{n}") for n in range(2)]
        y_stored = [sem(f"y_stored{n}") for n in range(2)]
        (setup_in, x_loaded, norm1_in, win_in, wout_in, xw_loaded, norm2_in, sample_rows_out, pages_in,
         lam_in) = [sem(n) for n in ("setup_in", "x_loaded", "norm1_in", "win_in", "wout_in", "xw_loaded",
                                     "norm2_in", "sample_rows_out", "pages_in", "lam_in")]
        (pool_consts, rstd_done, h_done, qk_copied, v_copied, eb_done, u_done, ss16_done, r16_done, rot_done,
         k_out, v_out, u_out, state_out, conv_done, sample_conv_done, vecs_done) = [sem(n) for n in (
             "pool_consts", "rstd_done", "h_done", "qk_copied", "v_copied", "eb_done", "u_done", "ss16_done",
             "r16_done", "rot_done", "k_out", "v_out", "u_out", "state_out", "conv_done", "sample_conv_done", "vecs_done")]
        (kmul_done, kred_done, pm_done, small_pe, gm_ready, sub_done, exp_done, es_done, pv_done, u_all,
         coef_done, us_done, qb_in, vn_in, sn_in, cmap_done) = [sem(n) for n in (
             "kmul_done", "kred_done", "pm_done", "small_pe", "gm_ready", "sub_done", "exp_done", "es_done",
             "pv_done", "u_all", "coef_done", "us_done", "qb_in", "vn_in", "sn_in", "cmap_done")]
        (max_done, pexp_done, comb_done, o_full, osq_done, oss_done, or_done, on_done) = [sem(n) for n in (
            "max_done", "pexp_done", "comb_done", "o_full", "osq_done", "oss_done", "or_done", "on_done")]
        (mean_done, zc_done, zsq_done, var_done, vr_done, zn_done, ez_done, mix_done, x2_done, h2_out,
         logits_done, logit_read, gexp_done, gexp_ask, gate_done, rank_done, rank_read, gT_done, gT_copied,
         bd_in, rw_in, x2_out) = [sem(n) for n in (
             "mean_done", "zc_done", "zsq_done", "var_done", "vr_done", "zn_done", "ez_done", "mix_done",
             "x2_done", "h2_out", "logits_done", "logit_read", "gexp_done", "gexp_ask", "gate_done",
             "rank_done", "rank_read", "gT_done", "gT_copied", "bd_in", "rw_in", "x2_out")]
        (ot_done, otsq_done, otss_done, otr_done) = [sem(n) for n in ("ot_done", "otsq_done", "otss_done",
                                                                      "otr_done")]
        (counts_done, addr_done, table_zeroed, table_written, table_in, meta_out, meta_in, bias_in,
         bias_split, fill_done, idx_done, gathered, y_scattered, pair_done) = [sem(n) for n in (
             "counts_done", "addr_done", "table_zeroed", "table_written", "table_in", "meta_out", "meta_in",
             "bias_in", "bias_split", "fill_done", "idx_done", "gathered", "y_scattered", "pair_done")]
        (xt_full, xt_copied, gclip_done, sig_done, act_done, at_full, at_copied, y_front, y_back,
         sel_done) = [sem(n) for n in ("xt_full", "xt_copied", "gclip_done", "sig_done",
                                       "act_done", "at_full", "at_copied", "y_front", "y_back", "sel_done")]
        act_step, dve_step, pool_step, dve_loop_step = [sem(n) for n in ("act_step", "dve_step", "pool_step",
                                                                         "dve_loop_step")]
        block = ctx.enter_context(nc.Block())

        def after(eng, s, value):
            if isinstance(value, int) and value <= 0:
                return
            eng.wait_ge(s, value)

        def t_view(bank, n):
            return bank[:, :].rearrange("p (i n) -> p i n", n=P)[:, :, 0:n]

        H_PARTS = [p for p in ORDER if USES[p[0]][2]]

        def after_h_tok_read(eng, part):
            no = base[part][2]
            if no:
                k = base[H_PARTS[no - 1]][1] + 1
                eng.wait_ge(t_full[k % 2], k // 2 + 1)
                if H_PARTS[no - 1][0] == "R":
                    eng.wait_ge(h2_out, 16 * (tail_no(H_PARTS[no - 1][1]) + 1))

        def after_h_T_read(eng, part):
            no = base[part][2]
            if no:
                kind, s = H_PARTS[no - 1]
                if kind == "P":
                    k = base[(kind, s)][0] + 4
                    eng.wait_ge(a_full[k % 2], k // 2 + 1)
                else:
                    eng.wait_ge(logits_done, tail_no(s) + 1)

        def pieces(s, dst, k):
            if s:
                return [(dst, A[k % 2][:, :])]
            return [(dst[:, q * P:(q + 1) * P], A[k % 2][32 * q:32 * q + NB, 0:P]) for q in range(4)]

        def filled(full, k):
            return full[k % 2], k // 2 + 1

        STEPS_OF = {"P": [1, 1] + [1.5] * 5 + [0.3] * 7, "Q": [0.5] * 15, "L": [1] * 4, "W": [1] * 4,
                    "R": [1] * 6}
        V_LAG = 3
        V_START = 5
        V_OF_STEP = {V_START: (), V_START + 1: (0, 1), **{V_START + g: (g,) for g in range(2, NG)}}

        def run_with_samples(step, mixer):
            steps = ((b, g) for b in range(-1, NB + 1) for g in range(NG if b < NB else V_START))
            due = 1
            for kind, stages in mixer:
                for n, _ in enumerate(stages):
                    while due >= 1:
                        for b, g in [x for x in [next(steps, None)] if x]:
                            step(b, g)
                        due -= 1
                    due += STEPS_OF[kind][n]
            for b, g in steps:
                step(b, g)

        w_slot = [wts[:, n * SLOT:(n + 1) * SLOT] for n in range(6)]
        CHUNK_SLOT = [2, 3, 4, 5, 0, 1]
        gu_chunk = [w_slot[CHUNK_SLOT[c]].rearrange("p (k n) -> p k n", k=2) for c in range(4)]
        dn_chunk = [w_slot[CHUNK_SLOT[4 + c]].rearrange("p (k n) -> p k n", k=4) for c in range(2)]

        @block.sync
        def _(sp):
            sp.dma_start(x_in[0:NB, :], x_rows[0]).then_inc(x_loaded, 16)
            sp.dma_start(norm_b[:, :], norm1_w[0].partition_broadcast(P)).then_inc(norm1_in, 16)
            for k in range(KT):
                sp.dma_start(w_in_sb[:, k, :], w_in[0, k * P:(k + 1) * P, :]).then_inc(win_in, 16)
            sp.wait_ge(pages_in, 16)

            page_regs = [sp.alloc_register(f"page{p}") for p in range(GP)]

            def load_pages(ring, full, cache, used, first_page, r, need):
                if need is not None:
                    sp.wait_ge(used, need)
                sp.load(page_regs, pages_sb[0:1, bass.ds(first_page, GP)])
                for p in range(GP):
                    page = sp.snap(page_regs[p], min_val=0, max_val=cache.shape[0] - 1)
                    sp.dma_start(ring[:, r, p, :],
                                 cache[bass.ds(page, 1)].rearrange("a p n -> (a p) n")).then_inc(full[r], 16)

            def load_q(b, even):
                sp.dma_start(q_b[:, 0 if even else 1, :],
                             q_rows[bass.ds(b, 1), :].rearrange("a n -> (a n)").partition_broadcast(P)
                             ).then_inc(qb_in, 16)

            def load_k(b, four, r, first=False):
                g = four * RING + r
                load_pages(k_ring, k_full, kc, kred_done, b * PAGES + g * GP, r,
                           None if first else b * NG + (g + 1 - RING))

            def load_v(b, four, r, wait=True):
                g = four * RING + (r - V_LAG)
                load_pages(v_ring, v_full, vc, pv_done, b * PAGES + g * GP, (r - V_LAG) % RING,
                           b * NG + (g + 1 - RING) if wait else None)

            def step(b, first=False, last=False):
                for half in range(2):
                    if first and half == 0:
                        for four in range(2):
                            for r in range(RING):
                                load_k(b + 1, four, r)
                                if four or r >= V_LAG:
                                    load_v(b, four, r, wait=four * RING + r - V_LAG >= RING)
                    else:
                        with sp.Fori(2 * half, 2 * half + 2) as four:
                            for r in range(RING):
                                if not last:
                                    load_k(b + 1, four, r)
                                load_v(b, four, r)
                    if half == 0:
                        if not first:
                            sp.wait_ge(u_all, b)
                        sp.dma_start(v_new[0:1, :], new_v_rows[0][bass.ds(b, 1), :]).then_inc(vn_in, 16)

            for r in range(RING):
                load_k(0, 0, r, True)
            sp.wait_ge(sample_rows_out, 64)
            load_q(0, True)
            load_q(1, False)
            with sp.Fori(1, NG // RING) as four:
                for r in range(RING):
                    load_k(0, four, r)
            step(0, first=True)
            with sp.Fori(0, (NB - 2) // 2) as pair:
                b = pair * 2 + 1
                for odd in range(2):
                    sp.wait_ge(kred_done, b * NG + odd * NG)
                    load_q(b + (odd + 1), odd == 0)
                    step(b + odd)
            step(NB - 1, last=True)
            for r in range(V_LAG):
                load_v(NB, 0, r)

            def load_chunk(c, e):
                if c < 4:
                    src = w_gate_up[0][bass.ds(e, 1), c * 256:(c + 1) * 256, :].rearrange(
                        "a (k p) n -> (a p) k n", p=P)
                    sp.dma_start(gu_chunk[c], src).then_inc(w_full[c], 16)
                else:
                    q = c - 4
                    src = w_down[0][bass.ds(e, 1), q * 512:(q + 1) * 512, :].rearrange(
                        "a (k p) n -> (a p) k n", p=P)
                    sp.dma_start(dn_chunk[q], src).then_inc(w_full[c], 16)

            def load_gate_up(i, e):
                for c in range(4):
                    sp.wait_ge(w_used[c], i)
                    load_chunk(c, e)

            def load_down(i, e):
                for c in range(4, 6):
                    sp.wait_ge(w_used[c], i)
                    load_chunk(c, e)

            k, n = filled(a_full, base[("P", TILES)][0] + 4)
            sp.wait_ge(k, n)
            for c in range(3):
                load_chunk(c, 0)
            sp.wait_ge(kred_done, NB * NG)
            load_chunk(3, 0)
            k, n = filled(a_full, base[("W", 0)][0] + 1)
            sp.wait_ge(k, n)
            for c in range(4, 6):
                load_chunk(c, 0)
            load_gate_up(1, 1)
            with sp.Fori(2, E) as i:
                load_gate_up(i, i)
                load_down(i - 1, i - 1)
            sp.wait_ge(meta_out, 1)
            n = sp.value_load(n_ovf[0:1, 0:1], min_val=0, max_val=OVF)
            with sp.Fori(0, OVF) as j:
                with sp.If(j < n):
                    e, e_before = [sp.value_load(e_tab[0:1, bass.ds(j + x, 1)], min_val=0, max_val=E - 1)
                                   for x in (E, E - 1)]
                    load_gate_up(j + E, e)
                    load_down(j + (E - 1), e_before)
            e = sp.value_load(e_tab[0:1, bass.ds(n + (E - 1), 1)], min_val=0, max_val=E - 1)
            load_down(n + (E - 1), e)

            sp.wait_ge(y_scattered, (n + E) * 16)
            sp.wait_ge(w_used[5], n + E)
            sp.wait_ge(x2_out, 16 * (TILES + 1))
            for u, s in enumerate(TAIL):
                m, b = rows_of(s), u % 2
                if u >= 2:
                    sp.wait_ge(y_stored[b], 16 * (u // 2))
                r = row0[s]
                sp.dma_start(out_rows[b][0:m, 0:TOPK * D],
                             y_rows[r * TOPK:(r + m) * TOPK, :].rearrange("(p k) n -> p (k n)", k=TOPK)
                             ).then_inc(y_loaded[b], 16)
                sp.dma_start(out_rows[b][0:m, TOPK * D:], x2_rows[r:r + m, :]).then_inc(y_loaded[b], 16)
            for u, s in enumerate(TAIL):
                m, b = rows_of(s), u % 2
                sp.wait_ge(y_stored[b], 16 * (u // 2 + 1))

        @block.gpsimd
        def _(pool):
            V = Chain(pool, pool_step)
            V.link(nc.gpsimd.memset(ident[:, :], 0.0))
            V.link(pool.affine_select(out=ident[:, :], in_=ident[:, :], compare_op=ALU.not_equal, fill=1.0,
                                      base=0, pattern=[[-1, P]], channel_multiplier=1))
            V.link(nc.gpsimd.memset(ones[:, :], 1.0))
            V.link(pool.affine_select(out=upper[:, :], in_=ones[:, :], compare_op=ALU.is_gt, fill=0.0,
                                      base=0, pattern=[[1, P]], channel_multiplier=-1))
            V.link(nc.gpsimd.memset(cmask[:, :], 0.0))
            V.link(pool.affine_select(out=cmask[:, :], in_=cmask[:, :], compare_op=ALU.is_ge, fill=NEG,
                                      base=0, pattern=[[-1, P]], channel_multiplier=1))
            V.link(nc.gpsimd.memset(eps_c[:, :], EPS))
            V.link(nc.gpsimd.memset(u_T[:, :, 0:TAPS - 1], 0.0))
            V.link(nc.gpsimd.memset(sc[:, :, PAGES, :], NEG))
            V.link(nc.gpsimd.memset(e_pad[:, :, :], 0.0))
            V.link(pool.iota(iota_e[:, :], [[1, E]], base=0, channel_multiplier=0,
                             allow_small_or_imprecise_dtypes=True))
            V.link(nc.gpsimd.memset(cmap[:, :, :], 0.0))
            for c in range(C):
                V.link(pool.affine_select(out=cmap[:, c, :], in_=cmap[:, c, :], compare_op=ALU.not_equal,
                                          fill=1.0, base=-c, pattern=[[-32, H]], channel_multiplier=1))
            pool.iota(iota_o[:, :], [[1, OVF + 1]], base=0, channel_multiplier=0,
                      allow_small_or_imprecise_dtypes=True).then_inc(pool_consts, 1)

            for s in range(1, TILES + 1):
                k, n = filled(t_free, base[("P", s)][1] + 4)
                pool.wait_ge(k, n)
                if s == 1:
                    pool.wait_ge(sample_conv_done, 1)
                    pool.wait_ge(sample_rows_out, 64)
                r = row0[s]
                z = mix_T[:, H:2 * H, r:r + P]
                for ct in range(CT):
                    V.link(nc.gpsimd.tensor_scalar(z[:, ct, :], u_T[:, ct, r:r + P], w_T[:, ct, 0:1],
                                                   vec_T[:, ct:ct + 1], ALU.mult, ALU.add))
                for j in range(1, TAPS):
                    w = w_T[:, :, j:j + 1].to_broadcast([P, CT, P])
                    V.link(nc.gpsimd.tensor_tensor(conv_tmpv, u_T[:, :, r + j:r + j + P], w, ALU.mult))
                    last = nc.gpsimd.tensor_tensor(z, z, conv_tmpv, ALU.add)
                    if j < TAPS - 1:
                        V.link(last)
                last.then_inc(conv_done, 1)
                pool.wait_ge(conv_done, s)

            k, n = filled(t_full, base[("Q", TILES)][1] + 4)
            pool.wait_ge(k, n)
            pool.wait_ge(v_out, 16 * TILES)
            V.link(pool.iota(fill_i, [[0, TCOLS]], base=UNUSED, channel_multiplier=TOPK))
            pool.dma_start(slot_table.rearrange("(p c) o -> p (c o)", c=TCOLS), fill_i).then_inc(table_zeroed, 16)
            V.link(pool.iota(pair_id.rearrange("p (t k) -> p t k", k=TOPK), [[TOPK * P, TILES + 1], [1, TOPK]],
                             base=0, channel_multiplier=TOPK))
            pool.wait_ge(table_zeroed, 16)
            pool.wait_ge(addr_done, 1)
            for u, s in enumerate(TAIL):
                m = rows_of(s)
                for kk in range(TOPK):
                    col = u * TOPK + kk
                    pool.indirect_dma_start(slot_table[:, :], bass.IndirectOffsetOnAxis(addr[0:m, col:col + 1], 0),
                                            pair_id[0:m, col:col + 1], None).then_inc(table_written, 16)
            pool.wait_ge(table_written, 16 * (TILES + 1) * TOPK)
            pool.dma_start(slots, slot_table.rearrange("(p c) o -> p (c o)", c=TCOLS)).then_inc(table_in, 16)

            bound, rows_0 = pool.alloc_register("bound"), pool.alloc_register("rows_0")
            pool.reg_mov(rows_0, 0)

            def gather(i, first):
                if not first:
                    pool.wait_ge(xt_full, i * 2)
                pool.wait_ge(idx_done, 1)
                V.link(nc.gpsimd.tensor_copy(g_idx, slot_tok[:, bass.ds(i, 1)]))
                pool.reg_add(bound, rows_0, TOK - 1)
                pool.indirect_dma_start(xg[:, :], None, h2_rows[:, :], bass.IndirectOffsetOnAxis(g_idx, 0),
                                        bounds_check=bound, oob_is_err=False).then_inc(gathered, 16)

            def scatter(i, first):
                pool.wait_ge(y_front, i + 1)
                pool.wait_ge(y_back, i + 1)
                if not first:
                    pool.wait_ge(y_scattered, i * 16)
                pool.wait_ge(table_in, 16)
                V.link(nc.gpsimd.tensor_copy(y_idx, slots[:, bass.ds(i, 1)]))
                pool.reg_add(bound, rows_0, PAIRS - 1)
                pool.indirect_dma_start(y_rows[:, :], bass.IndirectOffsetOnAxis(y_idx, 0), y_sb, None,
                                        bounds_check=bound, oob_is_err=False).then_inc(y_scattered, 16)

            pool.wait_ge(idx_done, 1)
            pool.wait_ge(h2_out, 16 * (TILES + 1))
            k, n = filled(t_full, base[("R", 0)][1] + 1)
            pool.wait_ge(k, n)
            gather(0, True)
            gather(1, False)
            gather(2, False)
            scatter(0, True)
            start = V.base + V.n
            with pool.Fori(2, E) as i:
                V.base, V.n = i * 2 + (start - 4), 0
                gather(i + 1, False)
                scatter(i - 1, False)
            pool.wait_ge(meta_out, 1)
            n = pool.value_load(n_ovf[0:1, 0:1], min_val=0, max_val=OVF)
            start += 2 * (E - 2)
            with pool.Fori(0, OVF) as j:
                with pool.If(j < n):
                    V.base, V.n = j * 2 + start, 0
                    gather(j + (E + 1), False)
                    scatter(j + (E - 1), False)
            V.base, V.n = n * 2 + start, 0
            scatter(n + (E - 1), False)

        @block.scalar
        def _(act):
            V = Chain(act, act_step)
            act.dma_start(pages_sb[:, :], page_table.rearrange("b n -> (b n)").rearrange("(a n) -> a n", a=1)
                          ).then_inc(pages_in, 16)
            for i, vec in enumerate((lambda_q1, lambda_k1, lambda_q2, lambda_k2)):
                act.dma_start(lam4[:, i, :], vec[0].partition_broadcast(P)).then_inc(lam_in, 16)
            n_in = [0]

            def small(dst, src):
                n_in[0] += 16
                act.dma_start(dst, src).then_inc(setup_in, 16)

            small(vecs[0:4, :], conv_b[0].rearrange("(c p) -> c p", p=P))
            small(vecs[4:8, :], conv_ln_g[0].rearrange("(c p) -> c p", p=P))
            small(vecs[8:12, :], conv_ln_b[0].rearrange("(c p) -> c p", p=P))
            small(vecs[12:13, :], subln_w)
            small(conv_w_in, conv_w[0])
            small(state_in,
                  state_conv[0].rearrange("(r b) j c -> (b j) r c", r=2))
            small(rope[:, 1:, :, :], rope_table[0:SEQ].rearrange("(t p) a n -> p t a n", p=P))
            small(rope[0:NB, 0, :, :], rope_table[SEQ:TOK])
            small(wqk[:, 0, :], q_norm_w[0].partition_broadcast(P))
            small(wqk[:, 1, :], k_norm_w[0].partition_broadcast(P))
            small(r_b[:, :], router_b[0].partition_broadcast(P))
            act.dma_start(new_conv_s[0, :, 0:TAPS - 2, :], state_conv[0, :, 1:TAPS - 1, :]).then_inc(state_out, 16)
            act.preload_act_table_set("natural_log_exp_and_others")
            act.wait_ge(pool_consts, 1)
            act.wait_ge(ss16_done, 1)
            nc.scalar.activation(stl[:, 4:6], stl[:, 2:4], ACT.Exp).then_inc(r16_done, 1)

            def rstd(out, tmp, ss, scale, signal):
                V.link(nc.scalar.activation(tmp, ss, ACT.Ln, bias=eps_c[0:ss.shape[0], :], scale=scale))
                nc.scalar.activation(out, tmp, ACT.Exp, scale=-0.5).then_inc(signal, 1)

            def normalise(part, src, n):
                after_h_tok_read(act, part)
                V.link(nc.scalar.activation(h_tok[0:n, :], src[0:n, :], ACT.Square, accum_out=stn[0:n, 0:1]))
                rstd(stn[0:n, 2:3], stn[0:n, 1:2], stn[0:n, 0:1], 1.0 / D, rstd_done)

            def copy_t(k, dst, src, scale=1.0):
                act.wait_ge(*filled(t_full, k))
                nc.scalar.activation(dst, src, ACT.Copy, scale=scale).then_inc(t_free[k % 2], 1)

            def copy_h(part, n):
                t0 = base[part][1]
                after_h_T_read(act, part)
                for q in range(2):
                    copy_t(t0 + q, h_T[:, 4 * q:4 * q + 4, 0:n], t_view(T[(t0 + q) % 2], n))

            def part_p(s):
                n, (a0, t0, _h) = rows_of(s), base[("P", s)]
                act.wait_ge(x_loaded, 16 * (s + 1))
                normalise(("P", s), x_in, n)
                yield
                act.wait_ge(h_done, base[("P", s)][2] + 1)
                if s < TILES:
                    act.dma_start(x_in[:, :], x_rows[s + 1]).then_inc(x_loaded, 16)
                else:
                    act.dma_start(norm_b[:, :], norm2_w[0].partition_broadcast(P)).then_inc(norm2_in, 16)
                copy_h(("P", s), n)
                yield
                for c in range(5):
                    yield
                    k = a0 + c
                    if c != 3:
                        act.wait_ge(*filled(a_full, k))
                    if c < 2:
                        after(act, rot_done, s)
                        after(act, comb_done, H * (s - 1))
                        for dst, src in pieces(s, qk[0:n, c * 512:(c + 1) * 512], k):
                            ins = nc.scalar.activation(dst, src, ACT.Copy)
                        ins.then_inc(a_free[k % 2], 1)
                    elif c == 2:
                        for dst, src in pieces(s, v_rows[s], k):
                            ins = nc.scalar.activation(dst, src, ACT.Copy)
                        ins.then_inc(a_free[k % 2], 1)
                        act.wait_ge(ss16_done, s + 2)
                        rstd(stp[0:n, 32:48], stp[0:n, 16:32], stp[0:n, 0:16], 1.0 / QD, r16_done)
                    elif c == 4:
                        if s:
                            act.wait_ge(*filled(t_full, base[("P", s - 1)][1] + (4 if s > 1 else 2)))
                            act.wait_ge(u_out, 16)
                        for dst, src in pieces(s, u_tok[0:n, :], k):
                            ins = nc.scalar.activation(dst, src, ACT.Exp, scale=-1.0)
                        ins.then_inc(a_free[k % 2], 1)
                    yield
                act.wait_ge(rot_done, s + 1)
                act.dma_start(new_k_rows[s], rot[0:n, AW:]).then_inc(k_out if s else sample_rows_out, 16)
                act.wait_ge(*filled(a_free, a0 + 2))
                act.dma_start(new_v_rows[s], v_rows[s]).then_inc(v_out if s else sample_rows_out, 16)
                if s:
                    cols = slice(row0[s], row0[s] + P)
                    copy_t(t0 + 2, q_T[:, :, cols], t_view(T[(t0 + 2) % 2], P))
                    copy_t(t0 + 3, k_T[:, :, cols], t_view(T[(t0 + 3) % 2], P))
                else:
                    act.dma_start(q_rows[:, :], rot[0:n, 0:AW]).then_inc(sample_rows_out, 16)
                    act.wait_ge(kmul_done, 1)
                    act.dma_start(s_new_rows[:, :], snw[0:n, :]).then_inc(sample_rows_out, 16)
                yield
                act.wait_ge(*filled(a_free, a0 + 3))
                if s == 0:
                    act.dma_start(new_conv_s[0, :, TAPS - 2, :], u_tok[0:n, :]).then_inc(u_out, 16)
                if s == TILES:
                    act.dma_start(new_conv_p[0, 0], u_tok[P - (TAPS - 1):P, :]).then_inc(u_out, 16)
                if s:
                    k = t0 + 4
                    copy_t(k, u_T[:, :, TAPS - 1 + row0[s]:TAPS - 1 + row0[s] + P], t_view(T[k % 2], P))
                else:
                    k = t0 + 2
                    copy_t(k, sext[:, :, :, TAPS - 1], t_view(T[k % 2], NB))
                    act.wait_ge(sample_rows_out, 64)
                    act.dma_start(s_new[:, :], s_new_rows.rearrange("b n -> (b n)").rearrange(
                        "(a n) -> a n", a=1)).then_inc(sn_in, 16)
                yield

            def part_c():
                t0 = base[("C", 0)][1]
                copy_t(t0, vec_T[:, 0:13], T[t0 % 2][:, 0:13])
                copy_t(t0 + 1, w_T[:, :, :], T[(t0 + 1) % 2][:, 0:CT * TAPS].rearrange("p (c j) -> p c j", c=CT))
                for r in range(2):
                    k = t0 + 2 + r
                    src = T[k % 2][:, 0:480].rearrange("p (c b j) -> p c b j", c=CT, b=4)
                    act.wait_ge(*filled(t_full, k))
                    for ct in range(CT):
                        ins = nc.scalar.activation(sext[:, ct, 4 * r:4 * r + 4, 0:TAPS - 1], src[:, ct], ACT.Copy)
                        if ct < CT - 1:
                            V.link(ins)
                    ins.then_inc(t_free[k % 2], 1)

            def part_q(s):
                t, (a0, t0, _h) = s - 1, base[("Q", s)]
                kw = (t + 1) * P
                for h in range(H):
                    yield
                    act.wait_ge(max_done, H * t + h + 1)
                    after(act, comb_done, H * t + h)
                    for c in range(C):
                        b = (a0 + 2 * h + c) % 2
                        nc.scalar.activation(exps[c][:, 0:kw], A[b][:, 0:kw], ACT.Exp, bias=stq[:, 2 + c:3 + c],
                                             scale=SM_SCALE, accum_out=stq[:, 4 + c:5 + c]
                                             ).then_inc(a_free[b], 1)
                    yield
                    k = t0 + h
                    after(act, o_full, H * t + h)
                    copy_t(k, a_T[:, 0:kw], T[k % 2][:, 0:kw])
                    yield
                act.wait_ge(o_full, H * (t + 1))
                act.wait_ge(*filled(t_full, t0 + H - 1))
                nc.scalar.activation(a_tok, O[:, :], ACT.Square).then_inc(osq_done, 1)
                yield
                act.wait_ge(oss_done, t + 1)
                rstd(stq[:, 16:20], stq[:, 12:16], stq[:, 8:12], 1.0 / VD, or_done)
                yield
                k = t0 + H
                copy_t(k, mix_T[:, 0:H, row0[s]:row0[s] + P], t_view(T[k % 2], P), scale=sub_w[:, :])
                yield

            ln_sq = [exps[0][:, :].rearrange("p (c n) -> p c n", c=CT), exps[1]]

            def part_l(s):
                u, n, r = tail_no(s), rows_of(s), row0[s]
                z = mix_T[:, H:2 * H, r:r + n]
                if u:
                    act.wait_ge(x2_out, 16 * u)
                act.dma_start(x2[0:n, :], x_rows[s]).then_inc(xw_loaded, 16)
                if u == 0:
                    act.dma_start(w_out_sb, w_out[0].rearrange("(k p) n -> p k n", p=P)).then_inc(wout_in, 16)
                    act.dma_start(bd, b_down[0]).then_inc(bd_in, 16)
                    act.dma_start(r_w, router_w[0].rearrange("(k p) n -> p k n", p=P)).then_inc(rw_in, 16)
                yield
                act.wait_ge(zc_done, u + 1)
                nc.scalar.activation(ln_sq[0][:, :, 0:n], z, ACT.Square).then_inc(zsq_done, 1)
                yield
                act.wait_ge(var_done, u + 1)
                rstd(ln_sq[1][:, P:P + n], ln_sq[1][:, 0:n], M[:, P:P + n], 1.0 / CH, vr_done)
                yield
                act.wait_ge(zn_done, u + 1)
                for ct in range(CT):
                    ins = nc.scalar.activation(ln_sq[0][:, ct, 0:n], z[:, ct, :], ACT.Exp,
                                               scale=neg_gb[:, ct:ct + 1], bias=neg_gb[:, CT + ct:CT + ct + 1])
                    if ct < CT - 1:
                        V.link(ins)
                ins.then_inc(ez_done, 1)
                yield

            def part_w(s):
                yield from [None] * 4

            def part_r(s):
                u, n, r, (a0, t0, hn) = tail_no(s), rows_of(s), row0[s], base[("R", s)]
                for c in range(2):
                    act.wait_ge(*filled(a_free, base[("W", s)][0] + c))
                normalise(("R", s), x2, n)
                yield
                act.wait_ge(h_done, hn + 1)
                act.dma_start(h2_rows[r:r + n, :], h_tok[0:n, :]).then_inc(h2_out, 16)
                copy_h(("R", s), n)
                yield
                yield
                act.wait_ge(gexp_ask, u + 1)
                nc.scalar.activation(str_[0:n, 4:8], top8[0:n, 0:TOPK], ACT.Exp, bias=str_[0:n, 0:1],
                                     accum_out=str_[0:n, 1:2]).then_inc(gexp_done, 1)
                yield
                yield
                for c in range(2):
                    act.wait_ge(*filled(a_free, a0 + c))
                act.dma_start(x2_rows[r:r + n, :], x2[0:n, :]).then_inc(x2_out, 16)
                yield

            def sample_step(b, g):
                if 0 <= b < NB and g == 4:
                    act.wait_ge(sub_done, b + 1)
                    after(act, u_all, b)
                    after(act, es_done, b)
                    nc.scalar.activation(ex[:, :, :], sc[:, b % 2, :, :], ACT.Exp, scale=SM_SCALE
                                         ).then_inc(exp_done, 1)

            for _ in part_p(0):
                pass
            part_c()
            parts = {"P": part_p, "Q": part_q, "L": part_l, "W": part_w, "R": part_r}
            run_with_samples(sample_step, [(kind, parts[kind](s)) for kind, s in ORDER[2:-4]])
            act.wait_ge(otsq_done, 1)
            rstd(sto[:, 0:32], sto[:, 32:64], M[:, 448:480], 1.0 / VD, otr_done)
            for kind, s in ORDER[-3:]:
                for _ in parts[kind](s):
                    pass

            k, v = filled(a_full, base[("W", 0)][0] + 1)
            act.wait_ge(k, v)
            for q in range(3):
                act.dma_start(b_stage[32 * q:32 * q + 32, :], b_gate_up[0]).then_inc(bias_in, 16)

            act.preload_act_table_set("sigmoid_and_others")
            def act_block(i, before=None):
                for part in range(2):
                    act.wait_ge(gclip_done, i * 2 + (part + 1))
                    after(act, act_done, i * 2 + (part - 1))
                    nc.scalar.activation(s_act[part], g_act[part], ACT.Sigmoid, scale=ALPHA
                                         ).then_inc(sig_done, 1)
                for part in range(2):
                    act.wait_ge(at_full, i * 2 + (part + 1))
                    nc.scalar.activation(act_T[part], t_view(TB[part], P), ACT.Copy).then_inc(at_copied, 1)
                copy_x(i + 1)
                if before is not None:
                    copy_y(before, i == 1 if isinstance(i, int) else False)

            def copy_x(i):
                for q in range(2):
                    act.wait_ge(xt_full, i * 2 + (q + 1))
                    nc.scalar.activation(hg_T[:, 4 * q:4 * q + 4, :], t_view(TB[q], P), ACT.Copy
                                         ).then_inc(xt_copied, 1)

            def copy_y(i, first):
                act.wait_ge(w_used[5], i + 1)
                if not first:
                    act.wait_ge(y_scattered, i * 16)
                for b in range(2):
                    for q in range(4):
                        m = nc.scalar.activation(y_sb[64 + 32 * b:96 + 32 * b, 256 * q:256 * (q + 1)],
                                                 PS[5][32 * q:32 * q + 32, 256 * b:256 * (b + 1)], ACT.Copy)
                m.then_inc(y_back, 1)

            TB = [PS[6], PS[7]]
            copy_x(0)
            act_block(0)
            act_block(1, 0)
            with act.Fori(2, E) as i:
                act_block(i, i - 1)
            act.wait_ge(meta_out, 1)
            n = act.value_load(n_ovf[0:1, 0:1], min_val=0, max_val=OVF)
            with act.Fori(0, OVF) as j:
                with act.If(j < n):
                    act_block(j + E, j + (E - 1))
            copy_y(n + (E - 1), False)
            for s, n in ((k_out, TILES), (v_out, TILES), (u_out, 2), (state_out, 1)):
                act.wait_ge(s, 16 * n)
            for u, s in enumerate(TAIL):
                m, b = rows_of(s), u % 2
                act.wait_ge(pair_done, TOPK * (u + 1))
                act.dma_start(y_out[s], out_rows[b][0:m, TOPK * D:]).then_inc(y_stored[b], 16)

        @block.tensor
        def _(pe):
            def fill_a(k):
                after(pe, a_free[k % 2], k // 2)

            def fill_t(k):
                after(pe, t_free[k % 2], k // 2)

            def transposes(k, src, n, count, cols=P):
                fill_t(k)
                for i in range(count):
                    m = pe.transpose(T[k % 2][0:cols, i * P:i * P + n], src[0:n, i * cols:(i + 1) * cols],
                                     ident[0:n, 0:n])
                m.then_inc(t_full[k % 2], 1)

            def transpose_h(part, n):
                t0, hn = base[part][1], base[part][2]
                pe.wait_ge(h_done, hn + 1)
                for q in range(2):
                    transposes(t0 + q, h_tok[:, 4 * q * P:(4 * q + 4) * P], n, 4)

            def part_p(s):
                n, (a0, t0, _h) = rows_of(s), base[("P", s)]
                yield
                transpose_h(("P", s), n)
                yield
                if s == 0:
                    pe.wait_ge(win_in, 16 * KT)
                for q in range(2):
                    pe.wait_ge(t_free[(t0 + q) % 2], (t0 + q) // 2 + 1)
                for c in range(5):
                    k = a0 + c
                    fill_a(k)
                    for kt in range(KT):
                        for q in range(1 if s else 4):
                            out, cols = (A[k % 2][:, :], 512) if s else (A[k % 2][32 * q:32 * q + NB, 0:P], P)
                            c0 = c * 512 + q * P
                            m = nc.tensor.matmul(out, h_T[:, kt, 0:n], w_in_sb[:, kt, c0:c0 + cols],
                                                 start=(kt == 0), stop=(kt == KT - 1))
                        if kt == KT - 1:
                            m.then_inc(a_full[k % 2], 1)
                        if kt % 4 == 3:
                            yield
                if s:
                    pe.wait_ge(rot_done, s + 1)
                    transposes(t0 + 2, rot[:, 0:AW], P, 4)
                    transposes(t0 + 3, rot[:, AW:], P, 4)
                yield
                k, v = filled(a_free, a0 + 3)
                pe.wait_ge(k, v)
                transposes(t0 + (4 if s else 2), u_tok, n, 4)
                yield

            def part_c():
                t0 = base[("C", 0)][1]
                pe.wait_ge(setup_in, 16 * 11)
                fill_t(t0)
                pe.transpose(T[t0 % 2][:, 0:13], vecs[0:13, :], ident[0:13, 0:13]).then_inc(t_full[t0 % 2], 1)
                k = t0 + 1
                fill_t(k)
                for ct in range(CT):
                    m = pe.transpose(T[k % 2][:, ct * TAPS:(ct + 1) * TAPS], conv_w_in[:, ct * P:(ct + 1) * P],
                                     ident[0:TAPS, 0:TAPS])
                m.then_inc(t_full[k % 2], 1)
                for r in range(2):
                    k = t0 + 2 + r
                    fill_t(k)
                    for ct in range(CT):
                        m = pe.transpose(T[k % 2][:, ct * 120:(ct + 1) * 120],
                                         state_in[:, r, ct * P:(ct + 1) * P], ident[0:120, 0:120])
                    m.then_inc(t_full[k % 2], 1)

            def values(s, h):
                t = s - 1
                k = base[("Q", s)][1] + h
                pe.wait_ge(t_free[k % 2], k // 2 + 1)
                if h == 0:
                    after(pe, on_done, t)
                for kb in range(t + 1):
                    m = nc.tensor.matmul(O[:, h * VD:(h + 1) * VD], a_T[:, kb * P:(kb + 1) * P],
                                         v_tok[:, kb, h * VD:(h + 1) * VD], start=(kb == 0), stop=(kb == t))
                m.then_inc(o_full, 1)

            def part_q(s):
                t, (a0, t0, _h) = s - 1, base[("Q", s)]
                kw = (t + 1) * P
                pe.wait_ge(*filled(t_free, base[("P", s)][1] + 2))
                pe.wait_ge(*filled(t_free, base[("P", s)][1] + 3))
                for h in range(H):
                    if h:
                        values(s, h - 1)
                    for c in range(C):
                        k = a0 + 2 * h + c
                        fill_a(k)
                        nc.tensor.matmul(A[k % 2][:, 0:kw], q_T[c * QD:(c + 1) * QD, h, t * P:(t + 1) * P],
                                         k_T[c * QD:(c + 1) * QD, h, 0:kw], start=True, stop=True
                                         ).then_inc(a_full[k % 2], 1)
                    yield
                    yield
                    pe.wait_ge(comb_done, H * t + h + 1)
                    transposes(t0 + h, a_tok, P, t + 1)
                    yield
                values(s, H - 1)
                yield
                yield
                pe.wait_ge(on_done, t + 1)
                transposes(t0 + H, a_tok, P, 4)
                yield

            def part_l(s):
                u, n, r = tail_no(s), rows_of(s), row0[s]
                z = mix_T[:, H:2 * H, r:r + n]
                if s:
                    pe.wait_ge(conv_done, s)
                else:
                    pe.wait_ge(sample_conv_done, 2)
                after(pe, zc_done, u)
                for ct in range(CT):
                    m = nc.tensor.matmul(M[:, 0:n], ones[:, :], z[:, ct, :], start=(ct == 0), stop=(ct == CT - 1))
                m.then_inc(mean_done, 1)
                yield
                yield
                pe.wait_ge(zsq_done, u + 1)
                sq = exps[0][:, :].rearrange("p (c n) -> p c n", c=CT)
                for ct in range(CT):
                    m = nc.tensor.matmul(M[:, P:P + n], ones[:, :], sq[:, ct, 0:n], start=(ct == 0),
                                         stop=(ct == CT - 1))
                m.then_inc(var_done, 1)
                yield
                yield

            def part_w(s):
                u, n, r, a0 = tail_no(s), rows_of(s), row0[s], base[("W", s)][0]
                pe.wait_ge(mix_done, u + 1)
                if u == 0:
                    pe.wait_ge(wout_in, 16)
                if s:
                    pe.wait_ge(*filled(t_free, base[("Q", s)][1] + H))
                for c in range(2):
                    k = a0 + c
                    fill_a(k)
                    for kt in range(KT):
                        m = nc.tensor.matmul(A[k % 2][0:n, :], mix_T[:, kt, r:r + n],
                                             w_out_sb[:, kt, c * 512:(c + 1) * 512],
                                             start=(kt == 0), stop=(kt == KT - 1))
                        if kt == KT - 1:
                            m.then_inc(a_full[k % 2], 1)
                        if kt % 4 == 3:
                            yield

            def part_r(s):
                u, n, (a0, t0, hn) = tail_no(s), rows_of(s), base[("R", s)]
                yield
                transpose_h(("R", s), n)
                yield
                for q in range(2):
                    pe.wait_ge(t_free[(t0 + q) % 2], (t0 + q) // 2 + 1)
                after(pe, logit_read, u)
                if u == 0:
                    pe.wait_ge(rw_in, 16)
                for kt in range(KT):
                    m = nc.tensor.matmul(M[0:n, 256:256 + E], h_T[:, kt, 0:n], r_w[:, kt, :],
                                         start=(kt == 0), stop=(kt == KT - 1))
                m.then_inc(logits_done, 1)
                yield
                yield
                pe.wait_ge(gate_done, u + 1)
                for v in range(u):
                    nc.tensor.matmul(M[0:n, 288:288 + E], ones[:, 0:n], chosen[:, v, :], start=(v == 0),
                                     stop=False)
                nc.tensor.matmul(M[0:n, 288:288 + E], upper[0:n, 0:n], chosen[0:n, u, :], start=(u == 0),
                                 stop=True).then_inc(rank_done, 1)
                pe.transpose(M[0:E, 320:320 + n], gsum[0:n, :], ident[0:n, 0:n]).then_inc(gT_done, 1)
                yield
                pe.wait_ge(gT_copied, u + 1)
                if u == 0:
                    pe.wait_ge(bd_in, 16)
                for c in range(2):
                    k = a0 + c
                    fill_a(k)
                    nc.tensor.matmul(A[k % 2][0:n, :], g_T[:, 0:n], bd[:, c * 512:(c + 1) * 512],
                                     start=True, stop=True).then_inc(a_full[k % 2], 1)
                yield

            def sample_out(b):
                pe.wait_ge(us_done, b + 1)
                nc.tensor.matmul(S7[:, 256 + 4 * b:260 + 4 * b], us[:, :], coef[:, :], start=True, stop=True
                                 ).then_inc(ot_done, 1)

            def sample_step(b, g):
                if 0 <= b < NB and g == 1:
                    pe.wait_ge(pm_done, b + 1)
                    pe.transpose(S7[0:HC, 0:P], pmax[:, :], ident[:, :]).then_inc(small_pe, 1)
                if 0 <= b < NB and g == 2:
                    pe.wait_ge(gm_ready, b + 1)
                    nc.tensor.matmul(S7[:, P:P + HC], ones[0:HC, :], dg[:, :], start=True, stop=True
                                     ).then_inc(small_pe, 1)
                if 0 < b < NB and g == 6:
                    sample_out(b - 1)
                if 0 <= b < NB and g == 7:
                    pe.wait_ge(es_done, b + 1)
                    nc.tensor.matmul(S7[:, P + HC:P + HC + 1], e_pad[:, :, :].rearrange("p h n -> p (h n)"),
                                     ones[:, 0:1], start=True, stop=True).then_inc(small_pe, 1)
                if g < V_START:
                    b, g = b - 1, g + NG
                if not 0 <= b < NB:
                    return
                for gg in V_OF_STEP[g]:
                    if gg == 0:
                        pe.wait_ge(exp_done, b + 1)
                        after(pe, us_done, b)
                    use = 4 * b + gg // RING + 1
                    pe.wait_ge(v_full[gg % RING], 16 * GP * use)
                    for p in range(GP):
                        page = gg * GP + p
                        for h in range(H):
                            m = nc.tensor.matmul(U[32 * h:32 * h + C, 0:VD], ex[:, page, C * h:C * h + C],
                                                 v_ring[:, gg % RING, p, h * VD:(h + 1) * VD],
                                                 start=(page == 0), stop=False)
                    m.then_inc(pv_done, 1)
                if g == NG - 1 + V_START:
                    pe.wait_ge(vn_in, 16 * (b + 1))
                    for h in range(H):
                        m = nc.tensor.matmul(U[32 * h:32 * h + C, 0:VD], ex[0:1, PAGES, C * h:C * h + C],
                                             v_new[0:1, h * VD:(h + 1) * VD], start=False, stop=True)
                    m.then_inc(u_all, 1)

            pe.wait_ge(pool_consts, 1)
            pe.wait_ge(cmap_done, 1)
            for _ in part_p(0):
                pass
            part_c()
            parts = {"P": part_p, "Q": part_q, "L": part_l, "W": part_w, "R": part_r}
            run_with_samples(sample_step, [(kind, parts[kind](s)) for kind, s in ORDER[2:-4]])
            sample_out(NB - 1)
            pe.wait_ge(otss_done, 1)
            nc.tensor.matmul(M[:, 448:480], ones[:, :], ot_sq[:, :], start=True, stop=True).then_inc(otsq_done, 1)
            for kind, s in ORDER[-3:]:
                for _ in parts[kind](s):
                    pass
            for v in range(TILES + 1):
                n = P if v < TILES else NB
                m = nc.tensor.matmul(M[:, 288:288 + E], ones[0:n, :], chosen[0:n, v, :], start=(v == 0),
                                     stop=(v == TILES))
            m.then_inc(counts_done, 1)

            TB = [PS[6], PS[7]]

            def transpose_x(i):
                pe.wait_ge(gathered, i * 16 + 16)
                for q in range(2):
                    if not (isinstance(i, int) and i == 0):
                        pe.wait_ge(at_copied, i * 2 + (q - 1))
                    for k in range(4):
                        m = pe.transpose(TB[q][:, k * P:(k + 1) * P], xg[:, (4 * q + k) * P:(4 * q + k + 1) * P],
                                         ident[:, :])
                    m.then_inc(xt_full, 1)

            def gate_up_products(lhs, rhs, backs, start, stop):
                for part in range(2):
                    for half in range(2):
                        m = nc.tensor.matmul(PS[part][64 * half:64 * half + 64, :], lhs[:, 0:64],
                                             rhs[:, part * F + half * 512:part * F + half * 512 + 512],
                                             start=start, stop=stop)
                for b in range(backs):
                    for part in range(2):
                        for half in range(2):
                            p0 = 64 * part + 32 * half
                            m = nc.tensor.matmul(PS[2 + b][p0:p0 + 32, :], lhs[:, 64 + 32 * b:96 + 32 * b],
                                                 rhs[:, part * F + half * 512:part * F + half * 512 + 512],
                                                 start=start, stop=stop)
                return m

            def gate_up(i, backs):
                gate_up_products(sel[0:96, :], b_split[0:96, :], backs, True, False)
                for c in range(4):
                    pe.wait_ge(w_full[c], i * 16 + 16)
                    for k in range(2):
                        m = gate_up_products(hg_T[:, 2 * c + k, :], gu_chunk[c][:, k, :], backs, False,
                                             c == 3 and k == 1)
                    m.then_inc(w_used[c], 1)

            def down(i, backs):
                for c in range(2):
                    pe.wait_ge(w_full[4 + c], i * 16 + 16)
                    for k in range(4):
                        w = dn_chunk[c][:, k, :]
                        first, last = c == 0 and k == 0, c == 1 and k == 3
                        for n in range(2):
                            m = nc.tensor.matmul(PS[4][64 * n:64 * n + 64, :], act_T[0][:, k, 64 * c:64 * c + 64],
                                                 w[:, n * 512:(n + 1) * 512], start=first, stop=last)
                        for b in range(backs):
                            a0 = 64 * b + 32 * c
                            for q in range(4):
                                m = nc.tensor.matmul(PS[5][32 * q:32 * q + 32, 256 * b:256 * (b + 1)],
                                                     act_T[1][:, k, a0:a0 + 32], w[:, q * 256:(q + 1) * 256],
                                                     start=first and b == 0,
                                                     stop=last and b == backs - 1)
                    m.then_inc(w_used[4 + c], 1)

            def by_size(work, i):
                size = pe.value_load(n_tok[0:1, bass.ds(i, 1)], min_val=0, max_val=CAP)
                with pe.If(size <= 64):
                    work(i, 0)
                with pe.If(size > 64):
                    with pe.If(size <= 96):
                        work(i, 1)
                    with pe.If(size > 96):
                        work(i, 2)

            def expert_block(i, before=None):
                after(pe, gclip_done, i * 2)
                pe.wait_ge(sel_done, i + 1)
                pe.wait_ge(xt_copied, i * 2 + 2)
                by_size(gate_up, i)
                if before is not None:
                    down_block(before, isinstance(i, int))
                for part in range(2):
                    pe.wait_ge(act_done, i * 2 + (part + 1))
                    for k in range(4):
                        m = pe.transpose(TB[part][:, k * P:(k + 1) * P], act_tok[part][:, k * P:(k + 1) * P],
                                         ident[:, :])
                    m.then_inc(at_full, 1)
                transpose_x(i + 1)

            def down_block(i, first):
                pe.wait_ge(at_copied, i * 2 + 2)
                if not first:
                    pe.wait_ge(y_front, i)
                    pe.wait_ge(y_back, i)
                by_size(down, i)

            transpose_x(0)
            pe.wait_ge(meta_out, 1)
            expert_block(0)
            expert_block(1, 0)
            with pe.Fori(2, E) as i:
                expert_block(i, i - 1)
            n = pe.value_load(n_ovf[0:1, 0:1], min_val=0, max_val=OVF)
            with pe.Fori(0, OVF) as j:
                with pe.If(j < n):
                    expert_block(j + E, j + (E - 1))
            down_block(n + (E - 1), False)

        @block.vector
        def _(dve):
            V = Chain(dve, dve_step)

            def add(out, a, b, op=ALU.add):
                return nc.vector.tensor_tensor(out, a, b, op)

            def mul(out, a, b):
                return nc.vector.tensor_tensor(out, a, b, ALU.mult)

            def total(out, src):
                return nc.vector.tensor_reduce(out, src, X, ALU.add)

            dve.wait_ge(lam_in, 64)
            pairs = lam4[:, :, :].rearrange("p (a b) n -> p a b n", a=2)
            V.link(mul(pairs[:, :, 0, :], pairs[:, :, 0, :], pairs[:, :, 1, :]))
            total(stl[:, 2:4], pairs[:, :, 0, :]).then_inc(ss16_done, 1)
            dve.wait_ge(pool_consts, 1)
            V.link(nc.vector.memset(U[:, :], 0.0))
            V.link(total(pad1[:, :], cmap[:, :, :].rearrange("p c h -> p (c h)")))
            V.link(nc.vector.tensor_scalar(pad1[:, :], pad1[:, :], -1.0, 1.0, ALU.mult, ALU.add))
            dve.wait_ge(r16_done, 1)
            V.link(add(nlam[:, :], stl[:, 5:6], stl[:, 4:5], ALU.subtract))
            V.link(nc.vector.tensor_scalar(nlam[:, :], nlam[:, :], -LAM_INIT, None, ALU.add))
            nc.vector.scalar_tensor_tensor(cmap[:, 0, :], cmap[:, 1, :], nlam[:, :], cmap[:, 0, :],
                                           ALU.mult, ALU.add).then_inc(cmap_done, 1)
            dve.wait_ge(norm1_in, 16)

            def scale_rows(part, src, n):
                hn = base[part][2]
                dve.wait_ge(rstd_done, hn + 1)
                nc.vector.scalar_tensor_tensor(h_tok[0:n, :], src[0:n, :], stn[0:n, 2:3], norm_b[0:n, :],
                                               ALU.mult, ALU.mult).then_inc(h_done, 1)

            def part_p(s):
                n, (a0, t0, _h) = rows_of(s), base[("P", s)]
                qk3 = qk[0:n, :].rearrange("p (g d) -> p g d", d=QD)
                rot3 = rot[0:n, :].rearrange("p (g d) -> p g d", d=QD)
                qk4 = qk[0:n, :].rearrange("p (a g d) -> p a g d", a=2, d=QD)
                rot4 = rot[0:n, :].rearrange("p (a g d) -> p a g d", a=2, d=QD)
                scale_rows(("P", s), x_in, n)
                yield
                yield
                yield from [None] * 3
                for c in range(2):
                    dve.wait_ge(*filled(a_free, a0 + c))
                if s == 1:
                    dve.wait_ge(sample_rows_out, 64)
                if s > 1:
                    dve.wait_ge(*filled(t_full, base[("Q", s - 1)][1] + H))
                    dve.wait_ge(o_full, H * (s - 1))
                V.link(mul(rot[0:n, :], qk[0:n, :], qk[0:n, :]))
                total(stp[0:n, 0:16], rot3).then_inc(ss16_done, 1)
                yield
                if s == 0:
                    dve.wait_ge(setup_in, 16 * 11)
                for i in range(2):
                    V.link(mul(cw[0:n, i, :].rearrange("p (a n) -> p a n", n=32),
                               rope[0:n, s, i:i + 1, :].to_broadcast([n, 4, 32]),
                               wqk[0:n, :, :].rearrange("p a (b n) -> p (a b) n", n=32)))
                yield
                dve.wait_ge(r16_done, s + 2)
                V.link(mul(qk3, qk3, stp[0:n, 32:48].unsqueeze(2).to_broadcast([n, 16, QD])))
                yield
                cos, sin = [cw[0:n, i, :].rearrange("p (a d) -> p a d", a=2).unsqueeze(2).to_broadcast(
                    [n, 2, HC, QD]) for i in range(2)]
                V.link(mul(rot4, qk4, cos))
                V.link(mul(qk4, qk4, sin))
                yield
                V.link(add(rot3[:, :, 0:32], rot3[:, :, 0:32], qk3[:, :, 32:64], ALU.subtract))
                add(rot3[:, :, 32:64], rot3[:, :, 32:64], qk3[:, :, 0:32]).then_inc(rot_done, 1)
                dve.wait_ge(rot_done, s + 1)
                if s == 0:
                    V.link(mul(qk[0:n, 0:AW], rot[0:n, 0:AW], rot[0:n, AW:]))
                    total(snw[0:n, :], qk3[:, 0:HC, :]).then_inc(kmul_done, 1)
                    dve.wait_ge(kmul_done, 1)
                yield
                yield
                dve.wait_ge(*filled(a_free, a0 + 4))
                V.link(nc.vector.tensor_scalar(u_tok[0:n, :], u_tok[0:n, :], 1.0, None, ALU.add))
                V.link(nc.vector.reciprocal(u_tok[0:n, :], u_tok[0:n, :]))
                dve.wait_ge(*filled(a_full, a0 + 3))
                k = a0 + 3
                if s:
                    mul(u_tok[0:n, :], A[k % 2][0:n, :], u_tok[0:n, :]).then_inc(a_free[k % 2], 1)
                else:
                    glu_a = v_tok[0:NB, 0, :]
                    for dst, src in pieces(s, glu_a, k):
                        V.link(nc.vector.tensor_copy(dst, src))
                    mul(u_tok[0:n, :], glu_a, u_tok[0:n, :]).then_inc(a_free[k % 2], 1)
                yield
                yield
                yield

            def part_c():
                t0 = base[("C", 0)][1]
                dve.wait_ge(*filled(t_free, t0))
                V.link(nc.vector.tensor_scalar(sub_w[:, :], vec_T[:, 12:13], 1.0 - LAM_INIT, None, ALU.mult))
                V.link(nc.vector.tensor_scalar(neg_gb[:, :], vec_T[:, 4:12], -1.0, None, ALU.mult))
                for k in (base[("P", 0)][1] + 2, t0 + 1, t0 + 2, t0 + 3):
                    dve.wait_ge(*filled(t_free, k))
                V.link(mul(sext, sext, w_T[:, :, :].unsqueeze(2).to_broadcast([P, CT, NB, TAPS])))
                V.link(total(zs[:, :, :], sext))
                add(zs[:, :, :], zs[:, :, :], vec_T[:, 0:4].unsqueeze(2).to_broadcast([P, CT, NB])
                    ).then_inc(sample_conv_done, 1)
                dve.wait_ge(sample_conv_done, 1)

            def part_q(s):
                t, (a0, t0, _h) = s - 1, base[("Q", s)]
                kw = (t + 1) * P
                for h in range(H):
                    for c in range(C):
                        k = a0 + 2 * h + c
                        dve.wait_ge(*filled(a_full, k))
                        diag = A[k % 2][:, t * P:(t + 1) * P]
                        V.link(add(diag, diag, cmask[:, :]))
                        V.link(nc.vector.reduce_max(stq[:, c:c + 1], A[k % 2][:, 0:kw], X))
                    nc.vector.tensor_scalar(stq[:, 2:4], stq[:, 0:2], -SM_SCALE, None, ALU.mult
                                            ).then_inc(max_done, 1)
                    yield
                    for c in range(C):
                        dve.wait_ge(*filled(a_free, a0 + 2 * h + c))
                    V.link(nc.vector.reciprocal(stq[:, 6:8], stq[:, 4:6]))
                    V.link(mul(stq[:, 7:8], stq[:, 7:8], nlam[:, :]))
                    if h:
                        dve.wait_ge(*filled(t_full, t0 + h - 1))
                    else:
                        dve.wait_ge(k_out, 16 * s)
                        for k in (2, 3):
                            dve.wait_ge(*filled(t_full, base[("P", s)][1] + k))
                    V.link(nc.vector.tensor_scalar(a_tok[:, 0:kw], exps[0][:, 0:kw], stq[:, 6:7], None, ALU.mult))
                    nc.vector.scalar_tensor_tensor(a_tok[:, 0:kw], exps[1][:, 0:kw], stq[:, 7:8], a_tok[:, 0:kw],
                                                   ALU.mult, ALU.add).then_inc(comb_done, 1)
                    yield
                    yield
                dve.wait_ge(osq_done, t + 1)
                total(stq[:, 8:12], a_tok.rearrange("p (h n) -> p h n", h=H)).then_inc(oss_done, 1)
                yield
                dve.wait_ge(or_done, t + 1)
                mul(a_tok.rearrange("p (h n) -> p h n", h=H), O[:, :].rearrange("p (h n) -> p h n", h=H),
                    stq[:, 16:20].unsqueeze(2).to_broadcast([P, H, VD])).then_inc(on_done, 1)
                yield
                yield

            def part_l(s):
                u, n, r = tail_no(s), rows_of(s), row0[s]
                z = mix_T[:, H:2 * H, r:r + n]
                e3 = exps[0][:, :].rearrange("p (c n) -> p c n", c=CT)[:, :, 0:n]
                dve.wait_ge(mean_done, u + 1)
                nc.vector.scalar_tensor_tensor(z, M[:, 0:n].unsqueeze(1).to_broadcast([P, CT, n]), -1.0 / CH, z,
                                               ALU.mult, ALU.add).then_inc(zc_done, 1)
                yield
                yield
                dve.wait_ge(vr_done, u + 1)
                mul(z, z, exps[1][:, P:P + n].unsqueeze(1).to_broadcast([P, CT, n])).then_inc(zn_done, 1)
                yield
                dve.wait_ge(ez_done, u + 1)
                for ct in range(CT):
                    V.link(nc.vector.tensor_scalar(z[:, ct, :], z[:, ct, :], vec_T[:, 4 + ct:5 + ct],
                                                   vec_T[:, 8 + ct:9 + ct], ALU.mult, ALU.add))
                V.link(nc.vector.tensor_scalar(e3, e3, 1.0, None, ALU.add))
                V.link(nc.vector.reciprocal(e3, e3))
                mul(z, z, e3).then_inc(mix_done, 1)
                yield

            def part_w(s):
                u, n, a0 = tail_no(s), rows_of(s), base[("W", s)][0]
                for c in range(2):
                    yield
                    k = a0 + c
                    dve.wait_ge(*filled(a_full, k))
                    if c == 0:
                        dve.wait_ge(xw_loaded, 16 * (u + 1))
                    cols = slice(c * 512, (c + 1) * 512)
                    add(x2[0:n, cols], x2[0:n, cols], A[k % 2][0:n, :]).then_inc(a_free[k % 2], 1)
                    yield

            def part_r(s):
                u, n, (a0, t0, hn) = tail_no(s), rows_of(s), base[("R", s)]
                if u == 0:
                    dve.wait_ge(norm2_in, 16)
                    V.link(nc.vector.memset(onehot[:, :, :, :], 0.0))
                    V.link(nc.vector.memset(rankk[:, :, :], 0.0))
                scale_rows(("R", s), x2, n)
                yield
                yield
                dve.wait_ge(logits_done, u + 1)
                add(logit[0:n, :], M[0:n, 256:256 + E], r_b[0:n, :]).then_inc(logit_read, 1)
                dve.wait_ge(logit_read, u + 1)
                V.link(nc.vector.max(top8[0:n, :], logit[0:n, :]))
                V.link(nc.vector.max_index(idx8[0:n, :], top8[0:n, :], logit[0:n, :]))
                V.link(nc.vector.tensor_copy(idxf[0:n, :], idx8[0:n, :]))
                nc.vector.tensor_scalar(str_[0:n, 0:1], top8[0:n, 0:1], -1.0, None, ALU.mult).then_inc(gexp_ask, 1)
                yield
                dve.wait_ge(gexp_done, u + 1)
                V.link(nc.vector.reciprocal(str_[0:n, 2:3], str_[0:n, 1:2]))
                V.link(nc.vector.tensor_scalar(gates[0:n, u, :], str_[0:n, 4:8], str_[0:n, 2:3], None, ALU.mult))
                for k in range(TOPK):
                    V.link(nc.vector.tensor_scalar(onehot[0:n, u, k, :], iota_e[0:n, :], idxf[0:n, k:k + 1], None,
                                                   ALU.is_equal))
                V.link(total(chosen[0:n, u, :], onehot[0:n, u, :, :].rearrange("p k e -> p e k")))
                V.link(mul(gtmp[0:n, :, :], onehot[0:n, u, :, :],
                           gates[0:n, u, :].unsqueeze(2).to_broadcast([n, TOPK, E])))
                total(gsum[0:n, :], gtmp[0:n, :, :].rearrange("p k e -> p e k")).then_inc(gate_done, 1)
                yield
                dve.wait_ge(rank_done, u + 1)
                dve.wait_ge(gate_done, u + 1)
                dve.wait_ge(gT_done, u + 1)
                V.link(mul(gtmp[0:n, :, :], onehot[0:n, u, :, :],
                           M[0:n, 288:288 + E].unsqueeze(1).to_broadcast([n, TOPK, E])))
                V.link(total(rankk[0:n, u, :], gtmp[0:n, :, :]))
                nc.vector.tensor_copy(g_T[:, 0:n], M[0:E, 320:320 + n]).then_inc(gT_copied, 1)
                yield
                for c in range(2):
                    k = a0 + c
                    dve.wait_ge(*filled(a_full, k))
                    cols = slice(c * 512, (c + 1) * 512)
                    add(x2[0:n, cols], x2[0:n, cols], A[k % 2][0:n, :]).then_inc(a_free[k % 2], 1)
                yield

            def sample_step(b, g):
                kb = b + 1
                if kb < NB:
                    r = g % RING
                    if g == 0:
                        dve.wait_ge(qb_in, 32 if kb == 0 else 16 * (kb + 1))
                        if kb == 0:
                            dve.wait_ge(sn_in, 16)
                        V.link(nc.vector.tensor_copy(sc[0:1, kb % 2, PAGES, :], s_new[0:1, kb * HC:(kb + 1) * HC]))
                    dve.wait_ge(k_full[r], 16 * GP * (4 * kb + g // RING + 1))
                    V.link(mul(k_ring[:, r, :, :], k_ring[:, r, :, :],
                               q_b[:, kb % 2, :].unsqueeze(1).to_broadcast([P, GP, AW])))
                    total(sc[:, kb % 2, GP * g:GP * (g + 1), :],
                          k_ring[:, r, :, :].rearrange("p g (h d) -> p g h d", d=QD)).then_inc(kred_done, 1)
                    if g == NG - 1:
                        dve.wait_ge(kred_done, NG * (kb + 1))
                        if kb:
                            dve.wait_ge(small_pe, 3 * (kb - 1) + 1)
                        nc.vector.tensor_reduce(pmax[:, :], sc[:, kb % 2, :, :].rearrange("p g e -> p e g"), X,
                                                ALU.max).then_inc(pm_done, 1)
                if 0 <= b < NB and g == 1:
                    dve.wait_ge(small_pe, 3 * b + 1)
                    V.link(nc.vector.reduce_max(mx[:, :], S7[0:HC, 0:P], X))
                    nc.vector.tensor_scalar(dg[:, :], ident[0:HC, 0:HC], mx[:, :], None, ALU.mult
                                            ).then_inc(gm_ready, 1)
                if 0 <= b < NB and g == 3:
                    dve.wait_ge(small_pe, 3 * b + 2)
                    add(sc[:, b % 2, :, :], sc[:, b % 2, :, :],
                        S7[:, P:P + HC].unsqueeze(1).to_broadcast([P, PAGES + 1, HC]), ALU.subtract
                        ).then_inc(sub_done, 1)
                if 0 < b < NB and g == 5:
                    copy_u(b - 1)
                if 0 <= b < NB and g == 5:
                    dve.wait_ge(exp_done, b + 1)
                    if b:
                        dve.wait_ge(small_pe, 3 * b)
                    total(e_pad[:, :, 0:C], ex[:, :, :].rearrange("p g (h c) -> p h c g", c=C)
                          ).then_inc(es_done, 1)
                if 0 <= b < NB and g == 8:
                    dve.wait_ge(small_pe, 3 * b + 3)
                    V.link(add(rl[:, :], S7[:, P + HC:P + HC + 1], pad1[:, :]))
                    V.link(nc.vector.reciprocal(rl[:, :], rl[:, :]))
                    if b:
                        dve.wait_ge(ot_done, b)
                    V.link(nc.vector.tensor_scalar(coef[:, :], cmap[:, 0, :], rl[:, :], None, ALU.mult))

            def copy_u(b):
                dve.wait_ge(u_all, b + 1)
                nc.vector.tensor_copy(us[:, :], U[:, 0:VD]).then_inc(us_done, 1)

            for _ in part_p(0):
                pass
            part_c()
            parts = {"P": part_p, "Q": part_q, "L": part_l, "W": part_w, "R": part_r}
            run_with_samples(sample_step, [(kind, parts[kind](s)) for kind, s in ORDER[2:-4]])
            copy_u(NB - 1)
            dve.wait_ge(ot_done, NB)
            V.link(nc.vector.tensor_copy(ot[:, :], S7[:, 256:256 + H * NB]))
            mul(ot_sq[:, :], ot[:, :], ot[:, :]).then_inc(otss_done, 1)
            V.link(nc.vector.tensor_copy(mix_T[:, H:2 * H, SEQ:TOK], zs[:, :, :]))
            dve.wait_ge(otr_done, 1)
            V.link(mul(ot[:, :], ot[:, :], sto[:, 0:H * NB]))
            nc.vector.tensor_scalar(mix_T[:, 0:H, SEQ:TOK], ot[:, :].rearrange("p (b h) -> p h b", h=H),
                                    sub_w[:, :], None, ALU.mult).then_inc(sample_conv_done, 1)
            for kind, s in ORDER[-3:]:
                for _ in parts[kind](s):
                    pass

            dve.wait_ge(counts_done, 1)
            c0, c1, c2 = cnt[:, 0, :], cnt[:, 1, :], cnt[:, 2, :]
            V.link(nc.vector.tensor_copy(c0, M[:, 288:288 + E]))
            V.link(nc.vector.tensor_scalar(c1, c0, float(CAP), None, ALU.is_gt))
            for m in range(2, -(-TOK // CAP)):
                V.link(nc.vector.scalar_tensor_tensor(c1, c0, float(m * CAP), c1, ALU.is_gt, ALU.add))
            V.link(nc.vector.tensor_tensor_scan(c2, ones[:, 0:E], c1, 0.0, ALU.mult, ALU.add))
            V.link(add(c1, c2, c1, ALU.subtract))
            TT5 = TILES + 1
            all_k = [P, TT5 * TOPK, E]
            oh = onehot[:, :, :, :].rearrange("p t k e -> p (t k) e")
            rk = rankk[:, :, :].rearrange("p t k -> p (t k)")
            V.link(mul(big, oh, c1.unsqueeze(1).to_broadcast(all_k)))
            V.link(total(ad[:, 0, :], big))
            V.link(mul(big, oh, iota_e[:, :].unsqueeze(1).to_broadcast(all_k)))
            V.link(total(ad[:, 1, :], big))
            V.link(nc.vector.tensor_scalar(ad[:, 2, :], rk, float(CAP), None, ALU.is_ge))
            V.link(nc.vector.tensor_copy(ad[:, 3, :], ad[:, 2, :]))
            for m in range(2, -(-TOK // CAP)):
                V.link(nc.vector.scalar_tensor_tensor(ad[:, 2, :], rk, float(m * CAP), ad[:, 2, :],
                                                      ALU.is_ge, ALU.add))
            V.link(add(ad[:, 0, :], ad[:, 0, :], ad[:, 2, :]))
            V.link(add(ad[:, 0, :], ad[:, 0, :], ad[:, 1, :], ALU.subtract))
            V.link(nc.vector.scalar_tensor_tensor(ad[:, 0, :], ad[:, 0, :], float(E - 1), ad[:, 3, :],
                                                  ALU.add, ALU.mult))
            V.link(add(ad[:, 0, :], ad[:, 0, :], ad[:, 1, :]))
            V.link(nc.vector.scalar_tensor_tensor(ad[:, 2, :], ad[:, 2, :], float(-CAP), rk, ALU.mult, ALU.add))
            V.link(nc.vector.scalar_tensor_tensor(ad[:, 0, :], ad[:, 2, :], float(TCOLS), ad[:, 0, :],
                                                  ALU.mult, ALU.add))
            dve.wait_ge(v_out, 16 * TILES)
            dve.wait_ge(table_zeroed, 16)
            nc.vector.tensor_copy(addr, ad[:, 0, :]).then_inc(addr_done, 1)
            ec = big[0:1, 0:OVF + 1, :]
            V.link(nc.vector.tensor_tensor(ec, c2[0:1, :].unsqueeze(1).to_broadcast([1, OVF + 1, E]),
                                           iota_o[0:1, :].unsqueeze(2).to_broadcast([1, OVF + 1, E]), ALU.is_le))
            V.link(total(ef[0:1, E:TCOLS], ec))
            V.link(nc.vector.tensor_scalar(ef[0:1, E:TCOLS], ef[0:1, E:TCOLS], float(E - 1), None, ALU.min))
            V.link(nc.vector.tensor_copy(ef[0:1, 0:E], iota_e[0:1, :]))
            V.link(nc.vector.tensor_copy(e_tab, ef[0:1, :]))
            V.link(nc.vector.tensor_copy(n_tok[:, 0:E], c0[0:1, :]))
            V.link(nc.vector.tensor_scalar(n_tok[:, 0:E], n_tok[:, 0:E], CAP, None, ALU.min))
            V.link(nc.vector.tensor_scalar(n_tok[:, E:TCOLS], n_tok[:, 0:TCOLS - E], 0, CAP, ALU.mult, ALU.add))
            nc.vector.tensor_copy(n_ovf, c2[0:1, E - 1:E]).then_inc(meta_out, 1)
            dve.wait_ge(meta_out, 1)

            dve.wait_ge(bias_in, 48)
            V.link(nc.vector.tensor_copy(b_split[0:96, :], b_stage[0:96, :]))
            V.link(add(b_stage[0:96, :], b_stage[0:96, :], b_split[0:96, :], ALU.subtract))
            V.link(nc.vector.tensor_copy(b_split[32:64, :], b_stage[32:64, :]))
            V.link(nc.vector.tensor_copy(b_split[64:96, :], b_stage[64:96, :]))
            V.link(add(b_stage[64:96, :], b_stage[64:96, :], b_split[64:96, :], ALU.subtract))
            V.link(nc.vector.tensor_copy(b_split[64:96, :], b_stage[64:96, :]))
            for q in range(3):
                V.link(nc.vector.tensor_copy(pick3[32 * q:32 * q + 32, :], ident[32 * q:32 * q + 32,
                                                                              32 * q:32 * q + 32]))

            STEPS = 7

            def select(i):
                e = dve.value_load(e_tab[0:1, bass.ds(i, 1)], min_val=0, max_val=E - 1)
                nc.vector.tensor_copy(sel[0:96, :], pick3[0:96, bass.ds(e, 1)].to_broadcast([96, P])
                                      ).then_inc(sel_done, 1)

            select(0)
            dve.wait_ge(table_in, 16)
            nc.vector.tensor_scalar(slot_tok, slots, 2, None, ALU.logical_shift_right).then_inc(idx_done, 1)

            def expert_block(i, before=None):
                dve.wait_ge(w_used[3], i + 1)
                sources = [[(g_act[0], u_act[0], PS[0][:, :], PS[1][:, :])],
                           [(g_act[1][64 * b:64 * b + 64, :], u_act[1][64 * b:64 * b + 64, :],
                             PS[2 + b][0:64, :], PS[2 + b][64:128, :]) for b in range(2)]]
                for part in range(2):
                    for g_out, u_out, g, u in sources[part]:
                        V.link(nc.vector.tensor_scalar(g_out, g, LIMIT, None, ALU.min))
                        last = nc.vector.tensor_scalar(u_out, u, LIMIT, -LIMIT, ALU.min, ALU.max)
                        if g_out is not sources[part][-1][0]:
                            V.link(last)
                    last.then_inc(gclip_done, 1)
                for part in range(2):
                    dve.wait_ge(gclip_done, i * 2 + (part + 1))
                    V.link(nc.vector.scalar_tensor_tensor(u_act[part], u_act[part], 1.0, g_act[part],
                                                          ALU.add, ALU.mult))
                    dve.wait_ge(sig_done, i * 2 + (part + 1))
                    after(dve, at_full, i * 2 + (part - 1))
                    mul(act_tok[part], u_act[part], s_act[part]).then_inc(act_done, 1)
                    dve.wait_ge(act_done, i * 2 + (part + 1))
                select(i + 1)
                if before is not None:
                    copy_y(before, isinstance(i, int))

            def copy_y(i, first):
                dve.wait_ge(w_used[5], i + 1)
                if not first:
                    dve.wait_ge(y_scattered, i * 16)
                V.link(nc.vector.tensor_copy(y_sb[0:64, 0:512], PS[4][0:64, :]))
                nc.vector.tensor_copy(y_sb[0:64, 512:], PS[4][64:128, :]).then_inc(y_front, 1)

            expert_block(0)
            expert_block(1, 0)
            start = V.base + V.n
            V.base, V.n = start, 0
            with dve.Fori(2, E) as i:
                V.base = (i - 2) * STEPS + start
                V.n = 0
                expert_block(i, i - 1)
                assert V.n == STEPS
            n = dve.value_load(n_ovf[0:1, 0:1], min_val=0, max_val=OVF)
            start += (E - 2) * STEPS
            with dve.Fori(0, OVF) as j:
                with dve.If(j < n):
                    V.base, V.n = j * STEPS + start, 0
                    expert_block(j + E, j + (E - 1))
            V.base, V.n = n * STEPS + start, 0
            copy_y(n + (E - 1), False)

            for u, s in enumerate(TAIL):
                m, b = rows_of(s), u % 2
                dve.wait_ge(y_loaded[b], 32 * (u // 2 + 1))
                acc = out_rows[b][0:m, TOPK * D:]
                for k in range(TOPK):
                    nc.vector.scalar_tensor_tensor(acc, out_rows[b][0:m, k * D:(k + 1) * D], gates[0:m, u, k:k + 1],
                                                   acc, ALU.mult, ALU.add).then_inc(pair_done, 1)
                    dve.wait_ge(pair_done, u * TOPK + k + 1)


_INS = ["x_prompt", "x_sample", "cache_k", "cache_v", "state_conv", "page_table", "norm1_w", "w_in", "q_norm_w",
        "k_norm_w", "lambda_q1", "lambda_k1", "lambda_q2", "lambda_k2", "subln_w", "conv_w", "conv_b", "conv_ln_g",
        "conv_ln_b", "w_out", "norm2_w", "router_w", "router_b", "w_gate_up", "b_gate_up", "w_down", "b_down"]
_OUTS = [(1, 512, 1024), (8, 1, 1024), (1, 1, 512, 4, 2, 64), (1, 1, 512, 4, 128), (1, 1, 30, 512),
         (1, 8, 1, 4, 2, 64), (1, 8, 1, 4, 128), (1, 8, 30, 512)]


def _rope_table():
    half = QD // 2
    inv = np.power(np.float32(10000.0), -np.arange(half, dtype=np.float32) / np.float32(half)).astype(np.float32)
    pos = np.concatenate([np.arange(SEQ), np.full(NB, PAGES * PAGE)]).astype(np.float32)
    ang = (pos[:, None] * inv[None, :]).astype(np.float32)
    return np.stack([np.cos(ang), np.sin(ang)], axis=1).astype(np.float32)


def kernel(**inputs):
    import numpy as _np
    import concourse.bacc as _bacc
    from concourse import mybir as _mybir
    from concourse.bass_utils import run_bass_kernel_spmd as _run

    nc = _bacc.Bacc("TRN2", target_bir_lowering=False, num_devices=1)
    arrays, args = {}, []
    for name in _INS:
        a = _np.ascontiguousarray(inputs[name])
        arrays[f"in_{name}"] = a
        args.append(nc.dram_tensor(f"in_{name}", a.shape, _mybir.dt.from_np(a.dtype), kind="ExternalInput").ap())
    table = _rope_table()
    arrays["rope_table"] = table
    fp32, i32 = _mybir.dt.float32, _mybir.dt.int32
    args.append(nc.dram_tensor("rope_table", table.shape, fp32, kind="ExternalInput").ap())
    for i, shape in enumerate(_OUTS):
        args.append(nc.dram_tensor(f"out_{i}", shape, fp32, kind="ExternalOutput").ap())
    for name, shape, dt in (("h2_rows", (TOK, D), fp32), ("x2_rows", (TOK, D), fp32), ("y_rows", (PAIRS, D), fp32),
                            ("q_rows", (NB, AW), fp32), ("s_new_rows", (NB, HC), fp32),
                            ("slot_table", (P * TCOLS, 1), i32)):
        args.append(nc.dram_tensor(name, shape, dt, kind="Internal").ap())
    hybrid_step(nc, *args)
    r = _run(nc, [arrays], core_ids=[0])
    return tuple(r.results[0][f"out_{i}"] for i in range(len(_OUTS)))
```
